# Optimizing a Trainium2 kernel written in Bass

```python
import math
import jax
import jax.numpy as jnp
from jax import lax
import numpy as np

D_MODEL = 1024
BATCH = 1
SEQ = 1024
DEPTH = 1

CTX_LEN = 256
GRID_W = 64
N_MIXERS = 4
GROUP_WIDTH = D_MODEL // N_MIXERS
HEAD_DIM = 64
N_HEADS = GROUP_WIDTH // HEAD_DIM
CHUNK = 64
CONV_K = 3
GLA_GATE_RANK = 16
GLA_GATE_NORM = 16.0
RWKV_DECAY_RANK = 32
RWKV_A_RANK = 32
RWKV_G_RANK = 64
RWKV_GN_EPS = 64e-5
SSM_STATE = 128
SSM_GROUPS = 2
SSM_HPG = N_HEADS // SSM_GROUPS
SSM_XBC = GROUP_WIDTH + 2 * SSM_GROUPS * SSM_STATE
N_EXPERTS = 64
TOP_K = 8
EXPERT_DIM = 256
SHARED_DIM = 256
ROUTED_SCALE = 2.5
MOE_BLOCK = 128
RMS_EPS = 1e-6

IN_SPLITS = (
    GROUP_WIDTH, GROUP_WIDTH, GROUP_WIDTH, GROUP_WIDTH, GLA_GATE_RANK, GLA_GATE_RANK,
    GROUP_WIDTH, GROUP_WIDTH, GROUP_WIDTH, RWKV_DECAY_RANK, RWKV_DECAY_RANK, RWKV_A_RANK, RWKV_G_RANK,
    GROUP_WIDTH, SSM_XBC, N_HEADS, N_HEADS,
    3 * GROUP_WIDTH, GROUP_WIDTH, N_HEADS, N_HEADS, N_HEADS, N_HEADS,
)
IN_WIDTH = sum(IN_SPLITS)

kernel_name = "hymba_style_bidir_hybrid_moe_block"

def rms_norm(x, g):
    xf = x.astype(jnp.float32)
    y = xf * lax.rsqrt(jnp.mean(xf * xf, axis=-1, keepdims=True) + RMS_EPS)
    return (y * g.astype(jnp.float32)).astype(x.dtype)

def modulate(x, g, shift, scale):
    return rms_norm(x, g) * (1 + scale) + shift

def split_heads(t, n=N_HEADS):
    return t.reshape(t.shape[:-1] + (n, t.shape[-1] // n)).astype(jnp.float32)

def merge_heads(t):
    return t.reshape(t.shape[:-2] + (-1,))

def l2norm(t, eps=1e-6):
    return t * lax.rsqrt(jnp.sum(t * t, axis=-1, keepdims=True) + eps)

def head_rms(o, g):
    o = o * lax.rsqrt(jnp.mean(o * o, axis=-1, keepdims=True) + RMS_EPS)
    return merge_heads(o * g.astype(jnp.float32).reshape(o.shape[-2:]))

def flip(t):
    return t[:, ::-1]

def to_chunks(t):
    b, l = t.shape[:2]
    t = t.reshape((b, l // CHUNK, CHUNK) + t.shape[2:])
    return jnp.swapaxes(t, 2, 3)

def from_chunks(t):
    t = jnp.swapaxes(t, 2, 3)
    return t.reshape((t.shape[0], t.shape[1] * t.shape[2]) + t.shape[3:])

def bidir(core, fwd_args, bwd_args, init):
    y_f, s_f = core(*fwd_args, init[0])
    y_b, s_b = core(*[flip(a) for a in bwd_args], init[1])
    return y_f + flip(y_b), (s_f, s_b)

def dwconv2d(u, w, rows, cols):
    b, l, ch = u.shape
    y = lax.conv_general_dilated(
        u.reshape(b, rows, cols, ch), w[:, :, None, :].astype(u.dtype), (1, 1), 'SAME',
        dimension_numbers=('NHWC', 'HWIO', 'NHWC'), feature_group_count=ch)
    return y.reshape(b, l, ch)

def zero_states(batch):
    z = lambda *s: jnp.zeros((batch, N_HEADS) + s, jnp.float32)
    pair = lambda *s: (z(*s), z(*s))
    return (pair(HEAD_DIM, HEAD_DIM), pair(HEAD_DIM, HEAD_DIM),
            pair(HEAD_DIM, SSM_STATE), pair(HEAD_DIM, HEAD_DIM))

def gla_core(q, k, v, gk, s0):
    incl = jnp.tril(jnp.ones((CHUNK, CHUNK), bool))
    q, k, v, gk = (to_chunks(t) for t in (q * q.shape[-1] ** -0.5, k, v, gk))
    b = jnp.cumsum(gk, axis=3)
    b_last = b[:, :, :, -1:]
    q_t = q * jnp.exp(b)
    k_t = k * jnp.exp(-b)
    k_s = k * jnp.exp(b_last - b)
    att = jnp.where(incl, jnp.einsum('bnhid,bnhjd->bnhij', q_t, k_t), 0.0)
    o_intra = jnp.einsum('bnhij,bnhjv->bnhiv', att, v)

    def step(s, xs):
        q_n, k_n, v_n, dec_n = xs
        o_n = jnp.einsum('bhid,bhdv->bhiv', q_n, s)
        s = s * dec_n[..., None] + jnp.einsum('bhjd,bhjv->bhdv', k_n, v_n)
        return s, o_n

    xs = tuple(jnp.moveaxis(t, 1, 0) for t in (q_t, k_s, v, jnp.exp(b_last[:, :, :, 0])))
    s_fin, o_inter = lax.scan(step, s0, xs)
    return from_chunks(o_intra + jnp.moveaxis(o_inter, 0, 1)), s_fin

def gla_mixer(q, k, v, g, gl_f, gl_b, lp, init):
    dt_in = g.dtype
    q, k, v = split_heads(q), split_heads(k), split_heads(v)

    def forget(gl, d):
        z = gl @ lp['gla_gate_w2'][d] + lp['gla_gate_b'][d]
        return split_heads(jax.nn.log_sigmoid(z.astype(jnp.float32))) / GLA_GATE_NORM

    o, st = bidir(gla_core, (q, k, v, forget(gl_f, 0)), (q, k, v, forget(gl_b, 1)), init)
    y = head_rms(o, lp['gla_norm_g']) * jax.nn.silu(g.astype(jnp.float32))
    return y.astype(dt_in), st

def rwkv_core(r, w, k, v, z, b, s0):
    def step(s, xs):
        r_t, w_t, k_t, v_t, z_t, b_t = xs
        sz = jnp.einsum('bhvk,bhk->bhv', s, z_t)
        s = (s * w_t[:, :, None, :] + sz[..., None] * b_t[:, :, None, :]
             + v_t[..., None] * k_t[:, :, None, :])
        return s, jnp.einsum('bhvk,bhk->bhv', s, r_t)

    s_fin, y = lax.scan(step, s0, tuple(jnp.moveaxis(t, 1, 0) for t in (r, w, k, v, z, b)))
    return jnp.moveaxis(y, 0, 1), s_fin

def rwkv_mixer(r, k, v, wl_f, wl_b, al, gl, lp, init):
    f32 = jnp.float32
    dt_in = r.dtype
    r, k, v = split_heads(r), split_heads(k), split_heads(v)

    def decay(wl, d):
        w = lp['rwkv_w0'][d] + jnp.tanh(wl) @ lp['rwkv_w_w2'][d]
        w = -jax.nn.softplus(-w.astype(f32)) - 0.5
        return split_heads(jnp.exp(-jnp.exp(w)))

    a = split_heads(jax.nn.sigmoid((lp['rwkv_a0'] + al @ lp['rwkv_a_w2']).astype(f32)))
    gate = (jax.nn.sigmoid(gl) @ lp['rwkv_g_w2']).astype(f32)
    kk = l2norm(k * split_heads(lp['rwkv_k_k']))
    k = k * (1.0 + (a - 1.0) * split_heads(lp['rwkv_k_a']))
    z, bvec = -kk, kk * a
    o, st = bidir(rwkv_core, (r, decay(wl_f, 0), k, v, z, bvec),
                  (r, decay(wl_b, 1), k, v, z, bvec), init)
    mu = jnp.mean(o, axis=-1, keepdims=True)
    var = jnp.mean(jnp.square(o - mu), axis=-1, keepdims=True)
    o = merge_heads((o - mu) * lax.rsqrt(var + RWKV_GN_EPS))
    o = o * lp['rwkv_ln_g'].astype(f32) + lp['rwkv_ln_b'].astype(f32)
    bonus = jnp.sum(r * k * lp['rwkv_r_k'].astype(f32), axis=-1, keepdims=True) * v
    y = (o + merge_heads(bonus)) * gate
    return y.astype(dt_in), st

def ssd_core(x, a, bm, cm, s0):
    incl = jnp.tril(jnp.ones((CHUNK, CHUNK), bool))
    xc, ac, bc, cc = (to_chunks(t) for t in (x, a, bm, cm))
    bn, nc = xc.shape[:2]
    acum = jnp.cumsum(ac, axis=-1)
    seg = acum[..., :, None] - acum[..., None, :]
    lmat = jnp.exp(jnp.where(incl, seg, -jnp.inf))
    cb = jnp.einsum('bngis,bngjs->bngij', cc, bc)
    xg = xc.reshape(bn, nc, SSM_GROUPS, SSM_HPG, CHUNK, HEAD_DIM)
    m = cb[:, :, :, None] * lmat.reshape(bn, nc, SSM_GROUPS, SSM_HPG, CHUNK, CHUNK)
    y_intra = jnp.einsum('bngkij,bngkjp->bngkip', m, xg)
    dte = jnp.exp(acum[..., -1:] - acum).reshape(bn, nc, SSM_GROUPS, SSM_HPG, CHUNK)
    cs = jnp.einsum('bngjs,bngkj,bngkjp->bngkps', bc, dte, xg)
    cs = cs.reshape(bn, nc, N_HEADS, HEAD_DIM, SSM_STATE)
    cd = jnp.exp(acum[..., -1])

    def step(s, xs):
        cs_n, cd_n = xs
        return s * cd_n[..., None, None] + cs_n, s

    s_fin, s_in = lax.scan(step, s0, (jnp.moveaxis(cs, 1, 0), jnp.moveaxis(cd, 1, 0)))
    s_in = jnp.moveaxis(s_in, 0, 1).reshape(bn, nc, SSM_GROUPS, SSM_HPG, HEAD_DIM, SSM_STATE)
    dec_in = jnp.exp(acum).reshape(bn, nc, SSM_GROUPS, SSM_HPG, CHUNK)
    y_off = jnp.einsum('bngis,bngkps->bngkip', cc, s_in) * dec_in[..., None]
    y = (y_intra + y_off).reshape(bn, nc, N_HEADS, CHUNK, HEAD_DIM)
    return from_chunks(y), s_fin

def mamba_mixer(z, xbc, dt_f, dt_b, lp, init, rows, cols):
    f32 = jnp.float32
    dt_in = z.dtype
    xbc = jax.nn.silu(dwconv2d(xbc, lp['ssm_conv_w'], rows, cols) + lp['ssm_conv_b'])
    xs, bm, cm = jnp.split(xbc, [GROUP_WIDTH, GROUP_WIDTH + SSM_GROUPS * SSM_STATE], axis=-1)
    xs = split_heads(xs)
    bm, cm = split_heads(bm, SSM_GROUPS), split_heads(cm, SSM_GROUPS)

    def discretise(dt_raw, d):
        dt = jax.nn.softplus((dt_raw + lp['ssm_dt_bias'][d]).astype(f32))
        return xs * dt[..., None], -jnp.exp(lp['ssm_A_log'][d].astype(f32)) * dt

    x_f, a_f = discretise(dt_f, 0)
    x_b, a_b = discretise(dt_b, 1)
    y, st = bidir(ssd_core, (x_f, a_f, bm, cm), (x_b, a_b, bm, cm), init)
    y = y + lp['ssm_D'].astype(f32)[:, None] * xs
    y = merge_heads(y) * jax.nn.silu(z.astype(f32))
    y = y.reshape(y.shape[:-1] + (SSM_GROUPS, -1))
    y = y * lax.rsqrt(jnp.mean(y * y, axis=-1, keepdims=True) + RMS_EPS)
    y = y.reshape(y.shape[:-2] + (GROUP_WIDTH,)) * lp['ssm_norm_g'].astype(f32)
    return y.astype(dt_in), st

def gdn_core(q, k, v, g, beta, s0):
    incl = jnp.tril(jnp.ones((CHUNK, CHUNK), bool))
    strict = jnp.tril(jnp.ones((CHUNK, CHUNK), bool), -1)
    q, k, v, g, beta = (to_chunks(t) for t in (q, k, v, g, beta))
    gcum = jnp.cumsum(g, axis=-1)
    seg = gcum[..., :, None] - gcum[..., None, :]
    kb = k * beta[..., None]
    a_kk = jnp.einsum('bnhid,bnhjd->bnhij', kb, k) * jnp.exp(jnp.where(strict, seg, -jnp.inf))
    rhs = jnp.concatenate([kb * jnp.exp(gcum)[..., None], v * beta[..., None]], axis=-1)
    sol = lax.linalg.triangular_solve(a_kk, rhs, left_side=True, lower=True, unit_diagonal=True)
    dk = k.shape[-1]
    w, u = sol[..., :dk], sol[..., dk:]
    a_qk = jnp.einsum('bnhid,bnhjd->bnhij', q, k) * jnp.exp(jnp.where(incl, seg, -jnp.inf))
    q_dec = q * jnp.exp(gcum)[..., None]
    k_dec = k * jnp.exp(gcum[..., -1:] - gcum)[..., None]
    g_last = jnp.exp(gcum[..., -1])

    def step(s, xs):
        w_n, u_n, aqk_n, q_n, k_n, gl_n = xs
        v_new = u_n - w_n @ s
        o_n = q_n @ s + aqk_n @ v_new
        s = s * gl_n[..., None, None] + jnp.swapaxes(k_n, -1, -2) @ v_new
        return s, o_n

    xs = tuple(jnp.moveaxis(t, 1, 0) for t in (w, u, a_qk, q_dec, k_dec, g_last))
    s_fin, o = lax.scan(step, s0, xs)
    return from_chunks(jnp.moveaxis(o, 0, 1)), s_fin

def deltanet_mixer(qkv, z, b_f, b_b, a_f, a_b, lp, init, rows, cols):
    f32 = jnp.float32
    dt_in = z.dtype
    qkv = jax.nn.silu(dwconv2d(qkv, lp['dn_conv_w'], rows, cols))
    q, k, v = (split_heads(t) for t in jnp.split(qkv, 3, axis=-1))
    q = l2norm(q) * HEAD_DIM ** -0.5
    k = l2norm(k)

    def gates(b_raw, a_raw, d):
        beta = jax.nn.sigmoid(b_raw.astype(f32))
        g = -jnp.exp(lp['dn_A_log'][d].astype(f32)) * jax.nn.softplus(
            (a_raw + lp['dn_dt_bias'][d]).astype(f32))
        return g, beta

    g_f, be_f = gates(b_f, a_f, 0)
    g_b, be_b = gates(b_b, a_b, 1)
    o, st = bidir(gdn_core, (q, k, v, g_f, be_f), (q, k, v, g_b, be_b), init)
    y = head_rms(o, lp['dn_norm_g']) * jax.nn.silu(z.astype(f32))
    return y.astype(dt_in), st

def mixer_block(h, init, lp, rows, cols):
    cuts = np.cumsum(IN_SPLITS)[:-1].tolist()
    (aq, ak, av, ag, agf, agb,
     br, bk, bv, bwf, bwb, ba, bg,
     cz, cxbc, cdf, cdb,
     dqkv, dz, dbf, dbb, daf, dab) = jnp.split(h @ lp['w_in'], cuts, axis=-1)
    ya, sa = gla_mixer(aq, ak, av, ag, agf, agb, lp, init[0])
    yb, sb = rwkv_mixer(br, bk, bv, bwf, bwb, ba, bg, lp, init[1])
    yc, sc = mamba_mixer(cz, cxbc, cdf, cdb, lp, init[2], rows, cols)
    yd, sd = deltanet_mixer(dqkv, dz, dbf, dbb, daf, dab, lp, init[3], rows, cols)
    y = jnp.concatenate([ya, yb, yc, yd], axis=-1) @ lp['w_out']
    return y, (sa, sb, sc, sd)

def swiglu(t, wg, wu, wd):
    return (jax.nn.silu(t @ wg) * (t @ wu)) @ wd

def moe_ffn(t, router_w, router_bias, w_gate, w_up, w_down, sh_gate, sh_up, sh_down):
    n_tok, d = t.shape
    n_assign = n_tok * TOP_K
    scores = jax.nn.sigmoid((t @ router_w).astype(jnp.float32))
    _, idx = lax.top_k(scores + router_bias.astype(jnp.float32), TOP_K)
    wts = jnp.take_along_axis(scores, idx, axis=-1)
    wts = wts / jnp.sum(wts, axis=-1, keepdims=True) * ROUTED_SCALE
    e_flat = idx.reshape(-1)
    order = jnp.argsort(e_flat)
    e_sorted = e_flat[order]
    tok_sorted = (order // TOP_K).astype(jnp.int32)
    w_sorted = wts.reshape(-1)[order]
    counts = jnp.bincount(e_flat, length=N_EXPERTS)
    padded = (counts + MOE_BLOCK - 1) // MOE_BLOCK * MOE_BLOCK
    start = jnp.cumsum(counts) - counts
    pend = jnp.cumsum(padded)
    pstart = pend - padded
    dest = pstart[e_sorted] + jnp.arange(n_assign) - start[e_sorted]
    n_blocks = -(-(n_assign + N_EXPERTS * (MOE_BLOCK - 1)) // MOE_BLOCK)
    buf_tok = jnp.zeros((n_blocks * MOE_BLOCK,), jnp.int32).at[dest].set(tok_sorted)
    buf_w = jnp.zeros((n_blocks * MOE_BLOCK,), jnp.float32).at[dest].set(w_sorted)
    blk_exp = jnp.minimum(
        jnp.searchsorted(pend, jnp.arange(n_blocks) * MOE_BLOCK, side='right'), N_EXPERTS - 1)

    def expert_block(args):
        tok, e = args
        return swiglu(t[tok], w_gate[e], w_up[e], w_down[e])

    y = lax.map(expert_block, (buf_tok.reshape(n_blocks, MOE_BLOCK), blk_exp))
    y = y.reshape(-1, d).astype(jnp.float32) * buf_w[:, None]
    routed = jnp.zeros((n_tok, d), jnp.float32).at[buf_tok].add(y)
    shared = swiglu(t, sh_gate, sh_up, sh_down).astype(jnp.float32)
    return (routed + shared).astype(t.dtype)

def setup_inputs(seed: int = 0) -> dict:
    key = jax.random.key(seed)
    keys = iter(jax.random.split(key, 48))
    f32 = jnp.float32

    def nrm(shape, scale):
        return jax.random.normal(next(keys), shape, f32) * scale

    def gain(shape):
        return 1.0 + nrm(shape, 0.05)

    def dt_bias(shape):
        dt = jnp.exp(jax.random.uniform(next(keys), shape, f32, math.log(1e-3), math.log(1e-1)))
        return dt + jnp.log(-jnp.expm1(-dt))

    def a_log(shape):
        return jnp.log(jax.random.uniform(next(keys), shape, f32, 1.0, 16.0))

    L, D, G = DEPTH, D_MODEL, GROUP_WIDTH
    return {
        'x': nrm((BATCH, SEQ, D), 1.0),
        'c': nrm((BATCH, D), 1.0),
        'ctx': nrm((BATCH, CTX_LEN, D), 1.0),
        'c_ctx': nrm((D,), 1.0),
        'norm1_g': gain((L, D)),
        'norm2_g': gain((L, D)),
        'w_mod': nrm((L, D, 6 * D), 0.5 * D ** -0.5),
        'b_mod': nrm((L, 6 * D), 0.02),
        'w_in': nrm((L, D, IN_WIDTH), D ** -0.5),
        'w_out': nrm((L, D, D), D ** -0.5),
        'gla_gate_w2': nrm((L, 2, GLA_GATE_RANK, G), GLA_GATE_RANK ** -0.5),
        'gla_gate_b': nrm((L, 2, G), 0.1),
        'gla_norm_g': gain((L, G)),
        'rwkv_w_w2': nrm((L, 2, RWKV_DECAY_RANK, G), 0.1),
        'rwkv_w0': -2.0 + nrm((L, 2, G), 1.0),
        'rwkv_a_w2': nrm((L, RWKV_A_RANK, G), RWKV_A_RANK ** -0.5),
        'rwkv_a0': nrm((L, G), 0.1),
        'rwkv_g_w2': nrm((L, RWKV_G_RANK, G), RWKV_G_RANK ** -0.5),
        'rwkv_k_k': 0.85 + nrm((L, G), 0.05),
        'rwkv_k_a': gain((L, G)),
        'rwkv_r_k': nrm((L, N_HEADS, HEAD_DIM), 0.1),
        'rwkv_ln_g': gain((L, G)),
        'rwkv_ln_b': nrm((L, G), 0.02),
        'ssm_conv_w': nrm((L, CONV_K, CONV_K, SSM_XBC), 1.0 / CONV_K),
        'ssm_conv_b': nrm((L, SSM_XBC), 0.02),
        'ssm_A_log': a_log((L, 2, N_HEADS)),
        'ssm_dt_bias': dt_bias((L, 2, N_HEADS)),
        'ssm_D': gain((L, N_HEADS)),
        'ssm_norm_g': gain((L, G)),
        'dn_conv_w': nrm((L, CONV_K, CONV_K, 3 * G), 1.0 / CONV_K),
        'dn_A_log': a_log((L, 2, N_HEADS)),
        'dn_dt_bias': dt_bias((L, 2, N_HEADS)),
        'dn_norm_g': gain((L, G)),
        'router_w': nrm((L, D, N_EXPERTS), D ** -0.5),
        'router_bias': nrm((L, N_EXPERTS), 0.01),
        'exp_w_gate': nrm((L, N_EXPERTS, D, EXPERT_DIM), D ** -0.5),
        'exp_w_up': nrm((L, N_EXPERTS, D, EXPERT_DIM), D ** -0.5),
        'exp_w_down': nrm((L, N_EXPERTS, EXPERT_DIM, D), EXPERT_DIM ** -0.5),
        'sh_w_gate': nrm((L, D, SHARED_DIM), D ** -0.5),
        'sh_w_up': nrm((L, D, SHARED_DIM), D ** -0.5),
        'sh_w_down': nrm((L, SHARED_DIM, D), SHARED_DIM ** -0.5),
        'final_norm_g': gain((D,)),
    }

def reference(x, c, ctx, c_ctx, norm1_g, norm2_g, w_mod, b_mod, w_in, w_out,
              gla_gate_w2, gla_gate_b, gla_norm_g,
              rwkv_w_w2, rwkv_w0, rwkv_a_w2, rwkv_a0, rwkv_g_w2, rwkv_k_k, rwkv_k_a,
              rwkv_r_k, rwkv_ln_g, rwkv_ln_b,
              ssm_conv_w, ssm_conv_b, ssm_A_log, ssm_dt_bias, ssm_D, ssm_norm_g,
              dn_conv_w, dn_A_log, dn_dt_bias, dn_norm_g,
              router_w, router_bias, exp_w_gate, exp_w_up, exp_w_down,
              sh_w_gate, sh_w_up, sh_w_down, final_norm_g):
    bsz, n_lat, d = x.shape
    rows = n_lat // GRID_W
    n_ctx = ctx.shape[1]
    ctx_init = zero_states(bsz)
    for i in range(DEPTH):
        last = i == DEPTH - 1
        lp = dict(
            w_in=w_in[i], w_out=w_out[i],
            gla_gate_w2=gla_gate_w2[i], gla_gate_b=gla_gate_b[i], gla_norm_g=gla_norm_g[i],
            rwkv_w_w2=rwkv_w_w2[i], rwkv_w0=rwkv_w0[i], rwkv_a_w2=rwkv_a_w2[i],
            rwkv_a0=rwkv_a0[i], rwkv_g_w2=rwkv_g_w2[i], rwkv_k_k=rwkv_k_k[i],
            rwkv_k_a=rwkv_k_a[i], rwkv_r_k=rwkv_r_k[i], rwkv_ln_g=rwkv_ln_g[i],
            rwkv_ln_b=rwkv_ln_b[i],
            ssm_conv_w=ssm_conv_w[i], ssm_conv_b=ssm_conv_b[i], ssm_A_log=ssm_A_log[i],
            ssm_dt_bias=ssm_dt_bias[i], ssm_D=ssm_D[i], ssm_norm_g=ssm_norm_g[i],
            dn_conv_w=dn_conv_w[i], dn_A_log=dn_A_log[i], dn_dt_bias=dn_dt_bias[i],
            dn_norm_g=dn_norm_g[i])
        mod_x = jax.nn.silu(c) @ w_mod[i] + b_mod[i]
        mod_c = jax.nn.silu(c_ctx) @ w_mod[i] + b_mod[i]
        sa_x, ca_x, ga_x, sf_x, cf_x, gf_x = jnp.split(mod_x[:, None, :], 6, axis=-1)
        sa_c, ca_c, ga_c, sf_c, cf_c, gf_c = jnp.split(mod_c[None, None, :], 6, axis=-1)
        y_c, ctx_states = mixer_block(modulate(ctx, norm1_g[i], sa_c, ca_c), ctx_init, lp, 1, n_ctx)
        y_x, _ = mixer_block(modulate(x, norm1_g[i], sa_x, ca_x), ctx_states, lp, rows, GRID_W)
        x = x + ga_x * y_x
        h_x = modulate(x, norm2_g[i], sf_x, cf_x).reshape(-1, d)
        moe_args = (router_w[i], router_bias[i], exp_w_gate[i], exp_w_up[i], exp_w_down[i],
                    sh_w_gate[i], sh_w_up[i], sh_w_down[i])
        if last:
            x = x + gf_x * moe_ffn(h_x, *moe_args).reshape(x.shape)
        else:
            ctx = ctx + ga_c * y_c
            h_c = modulate(ctx, norm2_g[i], sf_c, cf_c).reshape(-1, d)
            f = moe_ffn(jnp.concatenate([h_c, h_x], axis=0), *moe_args)
            ctx = ctx + gf_c * f[: bsz * n_ctx].reshape(ctx.shape)
            x = x + gf_x * f[bsz * n_ctx:].reshape(x.shape)
    return rms_norm(x, final_norm_g)


_drawn_inputs = setup_inputs


def setup_inputs(seed=0):
    import zlib

    import numpy as np

    out = dict(_drawn_inputs(seed))
    spreads = {}
    factors = {'ctx': 3.061,
     'c_ctx': 3.999,
     'gla_gate_b': 4.086,
     'gla_norm_g': 3.768,
     'rwkv_w_w2': 3.573,
     'rwkv_a0': 4.541,
     'rwkv_k_k': 20.653,
     'rwkv_k_a': 3.803,
     'rwkv_ln_g': 4.941,
     'rwkv_ln_b': 26.661,
     'ssm_conv_b': 4.059,
     'ssm_D': 18.272,
     'ssm_norm_g': 3.198,
     'dn_norm_g': 3.986}
    for name, (base, spread) in spreads.items():
        noise = np.random.default_rng([zlib.crc32(name.encode()), seed]).standard_normal(out[name].shape)
        drawn = base * np.exp(spread * noise) if base else spread * noise
        out[name] = jnp.asarray(drawn.astype(out[name].dtype))
    for name, factor in factors.items():
        out[name] = (out[name] * factor).astype(out[name].dtype)
    return out
```

```python
import concourse.bass as bass
from concourse import mybir
from contextlib import ExitStack

F32 = mybir.dt.float32
I32 = mybir.dt.int32
U32 = mybir.dt.uint32
ALU = mybir.AluOpType
ACT = mybir.ActivationFunctionType
AX = mybir.AxisListType

P = 128
D = 1024
KC = D // P
SEQ, CTX = 1024, 256
XT, CT = SEQ // P, CTX // P
NT = XT + CT
TOK = NT * P
GW = 256
NH, HD = 4, 64
GRID = 64
ROWS = SEQ // GRID
RMS_EPS = 1e-6
GN_EPS = 64e-5
NE, TOPK, ED = 64, 8, 256
NBLK = 128
BIG = 1e30

A_Q, A_G, A_GL = 0, 768, 1024
B_R, B_WL, B_GL = 1056, 1824, 1920
C_Z, C_XBC, C_DT = 1984, 2240, 3008
D_QKV, D_Z, D_BA = 3016, 3784, 4040


class Carve:

    def __init__(self, arena, at):
        self.arena, self.at = arena, at

    def take(self, *shape):
        n = 1
        for s in shape:
            n *= s
        view = self.arena[:, self.at:self.at + n]
        self.at += n
        assert self.at <= self.arena.shape[1], ("SBUF is full", self.at)
        if len(shape) == 2:
            view = view.rearrange("p (a b) -> p a b", a=shape[0])
        elif len(shape) == 3:
            view = view.rearrange("p (a b c) -> p a b c", a=shape[0], b=shape[1])
        elif len(shape) == 4:
            view = view.rearrange("p (a b c d) -> p a b c d", a=shape[0], b=shape[1], c=shape[2])
        return view


def hold(eng, sem, value):
    eng.wait_ge(sem, value)
    if not isinstance(value, int):
        eng.nop(nofuse=True)


class Chain:

    def __init__(self, eng, sem):
        self.eng, self.sem, self.n, self.shift = eng, sem, 0, 0

    def __call__(self, ins):
        self.n += 1
        ins.then_inc(self.sem, 1)
        hold(self.eng, self.sem, self.shift + self.n)

    def enter(self, i, per_trip):
        self.per_trip, self.start = per_trip, self.n
        self.shift = i * per_trip

    def leave(self, trips):
        assert self.n - self.start == self.per_trip, self.n - self.start
        self.n = self.start + self.per_trip * trips
        self.shift = 0


def heads(ap, h=NH):
    return ap.rearrange("p (h n) -> p h n", h=h)


def over(ap, n):
    return ap.unsqueeze(2).to_broadcast([ap.shape[0], ap.shape[1], n])


def each(ap, n):
    return ap.unsqueeze(1).to_broadcast([ap.shape[0], n, ap.shape[1]])


def rsqrt(nc, chain, x, y, t):
    chain(nc.vector.tensor_scalar(t.bitcast(I32), x.bitcast(I32), 1, None, ALU.arith_shift_right))
    chain(nc.vector.tensor_scalar(y.bitcast(I32), t.bitcast(I32), -1.0, float(0x5f3759df), ALU.mult, ALU.add))
    for _ in range(3):
        chain(nc.vector.tensor_tensor(t, y, y, ALU.mult))
        chain(nc.vector.scalar_tensor_tensor(t, t, -0.5, x, ALU.mult, ALU.mult))
        chain(nc.vector.scalar_tensor_tensor(y, t, 1.5, y, ALU.add, ALU.mult))


class Phase:

    def __init__(self, nc):
        self.nc, self.held = nc, []

    def semaphore(self, name):
        self.held.append(self.nc.alloc_semaphore(name))
        return self.held[-1]

    def __enter__(self):
        return self

    def __exit__(self, *failure):
        if failure[0] is None:
            self.nc.clear_and_free_semaphores(self.held)
            self.nc.all_engine_barrier()


class Kernel:
    pass


def constants(nc, k, ctx):
    made = ctx.semaphore("constants_made")
    v0 = ctx.semaphore("constants_base")
    with nc.Block() as block:
        @block.gpsimd
        def _(pool):
            n = 0
            todo = [(k.ident, 0.0), (k.ones, 1.0), (k.ge, 1.0), (k.gt, 1.0), (k.le, 1.0), (k.lt, 1.0),
                    (k.blk[16], 1.0), (k.blk[32], 1.0), (k.blk[64], 1.0)]
            for buf, value in todo:
                nc.gpsimd.memset(buf, value).then_inc(made, 1)
                n += 1
            pool.wait_ge(made, n)
            for buf, op, base, cm, step, fill in (
                    (k.ident, ALU.not_equal, 0, 1, -1, 1.0),
                    (k.ge, ALU.is_ge, 0, -1, 1, 0.0), (k.gt, ALU.is_gt, 0, -1, 1, 0.0),
                    (k.le, ALU.is_ge, 0, 1, -1, 0.0), (k.lt, ALU.is_gt, 0, 1, -1, 0.0)):
                nc.gpsimd.affine_select(out=buf, in_=buf, compare_op=op, fill=fill, base=base,
                                        pattern=[[step, P]], channel_multiplier=cm).then_inc(made, 1)
                n += 1
            for b in (16, 32, 64):
                v = k.blk[b].rearrange("p (n b) -> p n b", b=b)
                nc.gpsimd.affine_select(out=v, in_=v, compare_op=ALU.is_ge, fill=0.0, base=0,
                                        pattern=[[-b, P // b], [0, b]], channel_multiplier=1).then_inc(made, 1)
                n += 1
                pool.wait_ge(made, n)
                nc.gpsimd.affine_select(out=v, in_=v, compare_op=ALU.is_ge, fill=0.0, base=b - 1,
                                        pattern=[[b, P // b], [0, b]], channel_multiplier=-1).then_inc(made, 1)
                n += 1

            pool.wait_ge(made, n)
            TT = nc.gpsimd.tensor_tensor
            TT(k.lvl[32], k.blk[32], k.blk[16], ALU.subtract).then_inc(made, 1)
            TT(k.lvl[64], k.blk[64], k.blk[32], ALU.subtract).then_inc(made, 1)
            TT(k.lvl[128], k.ones, k.blk[64], ALU.subtract).then_inc(made, 1)
            for d in range(2):
                incl = k.incl[d]
                TT(k.glamask[d], incl, k.blk[64], ALU.mult).then_inc(made, 1)
                TT(k.dmask[d], k.strict[d], k.blk[16], ALU.mult).then_inc(made, 1)
                TT(k.dmaskT[d], k.strictT[d], k.blk[16], ALU.mult).then_inc(made, 1)
                nc.gpsimd.tensor_scalar(k.cap[d], incl, -1.0, BIG, ALU.add, ALU.mult).then_inc(made, 1)
                nc.gpsimd.tensor_scalar(k.floor[d], k.strict[d], -1.0, -BIG, ALU.add, ALU.mult).then_inc(made, 1)
                n += 5
            n += 3
            pool.wait_ge(made, n)
            for d in range(2):
                nc.gpsimd.tensor_scalar(k.glacum[d], k.glamask[d], 1.0 / 16.0, None, ALU.mult).then_inc(made, 1)
                n += 1
            pool.wait_ge(made, n)


def modulation(nc, k, ctx, cr, c, c_ctx, w_mod, b_mod, norm1_g, norm2_g):
    sem = lambda n: ctx.semaphore(n)
    loaded, gates_b, act_in = sem("mod_vectors_loaded"), sem("mod_gate_bias_loaded"), sem("silu_ready")
    w_in = [sem("w_mod_even_loaded"), sem("w_mod_odd_loaded")]
    done, colout, gateout, vch = sem("mod_section_done"), sem("mod_columns_out"), sem("mod_gates_out"), sem("mod_chain")
    cc = cr.take(2, KC)
    sc = cr.take(2, KC)
    bcol = cr.take(6, KC)
    gcol = cr.take(2, KC)
    modc = cr.take(6, KC, 2)
    W = cr.take(2, KC, D)
    PC, PG = k.ps[0], k.ps[1:3]
    wv = w_mod[0].rearrange("(p c) (s n) -> s p c n", c=KC, s=6)
    with nc.Block() as block:
        @block.sync
        def _(sp):
            sp.dma_start(cc[:, 0, :], c.rearrange("a (p c) -> p (a c)", c=KC)).then_inc(loaded, 16)
            sp.dma_start(cc[:, 1, :], c_ctx.rearrange("(p c) -> p c", c=KC)).then_inc(loaded, 16)
            sp.dma_start(bcol, b_mod.rearrange("a (s p c) -> p (a s) c", s=6, c=KC)).then_inc(loaded, 16)
            sp.dma_start(gcol[:, 0, :], norm1_g.rearrange("a (p c) -> p (a c)", c=KC)).then_inc(loaded, 16)
            sp.dma_start(gcol[:, 1, :], norm2_g.rearrange("a (p c) -> p (a c)", c=KC)).then_inc(loaded, 16)
            for n, s in enumerate((2, 5)):
                sp.dma_start(k.gate[n], b_mod[0:1, s * D:(s + 1) * D].to_broadcast([P, D])).then_inc(gates_b, 16)
            for s in range(6):
                if s >= 2:
                    sp.wait_ge(done, s - 1)
                sp.dma_start(W[:, s % 2], wv[s]).then_inc(w_in[s % 2], 16)

        @block.scalar
        def _(act):
            act.wait_ge(loaded, 80)
            nc.scalar.activation(sc, cc, ACT.Silu).then_inc(act_in, 1)

        @block.tensor
        def _(pe):
            pe.wait_ge(act_in, 1)
            for s in range(6):
                pe.wait_ge(w_in[s % 2], 16 * (s // 2 + 1))
                w = W[:, s % 2]
                if s in (2, 5):
                    if s == 5:
                        pe.wait_ge(gateout, 2)
                    for half in range(2):
                        for c_ in range(KC):
                            last = nc.tensor.matmul(PG[half][:, 0:512], sc[:, 0, c_:c_ + 1].to_broadcast([P, P]),
                                                    w[:, c_, half * 512:(half + 1) * 512],
                                                    start=(c_ == 0), stop=(c_ == KC - 1))
                else:
                    for m in range(KC):
                        at = (s * KC + m) * 2
                        for c_ in range(KC):
                            last = nc.tensor.matmul(PC[:, at:at + 2], w[:, c_, m::KC], sc[:, :, c_],
                                                    start=(c_ == 0), stop=(c_ == KC - 1))
                last.then_inc(done, 1)

        @block.vector
        def _(dve):
            chain = Chain(dve, vch)
            dve.wait_ge(gates_b, 32)
            for n, s in enumerate((2, 5)):
                dve.wait_ge(done, s + 1)
                for half in range(2):
                    g = k.gate[n][:, half * 512:(half + 1) * 512]
                    nc.vector.tensor_tensor(g, g, PG[half][:, 0:512], ALU.add).then_inc(gateout, 1)
            dve.wait_ge(loaded, 80)
            for s in (0, 1, 3, 4):
                ins = nc.vector.tensor_tensor(modc[:, s], PC[:, s * KC * 2:(s + 1) * KC * 2].rearrange(
                    "p (m j) -> p m j", j=2), over(bcol[:, s, :], 2), ALU.add)
                chain(ins)
            for n, (sh, scl) in enumerate(((0, 1), (3, 4))):
                for j in range(2):
                    if n == 1 and j == 1:
                        continue
                    nc.vector.scalar_tensor_tensor(k.mul_col[n][j], modc[:, scl, :, j], 1.0, gcol[:, n, :],
                                                   ALU.add, ALU.mult).then_inc(colout, 1)
                    nc.vector.tensor_copy(k.add_col[n][j], modc[:, sh, :, j]).then_inc(colout, 1)
            dve.wait_ge(colout, 6)


def normed_hidden(nc, k, ctx, cr, x, ctx_in):
    sem = lambda n: ctx.semaphore(n)
    x_in = [sem("x_even_loaded"), sem("x_odd_loaded")]
    sq, xn_ready, turned, vch = sem("squares_summed"), sem("xn_ready"), sem("x_turned"), sem("norm_chain")
    out = [sem("h_written_by_act"), sem("h_written_by_dve")]
    X = cr.take(2, D)
    XN = cr.take(2, D)
    junk = cr.take(2, D)
    ss = cr.take(2, 1)
    rs = cr.take(2, 1)
    ri = cr.take(2, 1)
    rt = cr.take(1)
    tiles = [ctx_in[0, t * P:(t + 1) * P, :] for t in range(CT)] + [x[0, t * P:(t + 1) * P, :] for t in range(XT)]
    with nc.Block() as block:
        @block.sync
        def _(sp):
            for t in range(NT):
                if t >= 2:
                    sp.wait_ge(xn_ready, t - 1)
                sp.dma_start(X[:, t % 2], tiles[t]).then_inc(x_in[t % 2], 16)

        @block.scalar
        def _(act):
            for t in range(NT + 1):
                if t < NT:
                    act.wait_ge(x_in[t % 2], 16 * (t // 2 + 1))
                    if t >= 2:
                        act.wait_ge(xn_ready, t - 1)
                    nc.scalar.activation(junk[:, t % 2], X[:, t % 2], ACT.Square,
                                         accum_out=ss[:, t % 2]).then_inc(sq, 1)
                if t >= 1:
                    u = t - 1
                    j = 1 if u < CT else 0
                    act.wait_ge(turned, u + 1)
                    for c in range(KC // 2):
                        nc.scalar.activation(k.hT[:, c, u * P:(u + 1) * P],
                                             k.ps[4 * (u % 2) + c // 4][:, (c % 4) * P:(c % 4 + 1) * P], ACT.Identity,
                                             bias=k.add_col[0][j][:, c:c + 1],
                                             scale=k.mul_col[0][j][:, c:c + 1]).then_inc(out[0], 1)

        @block.vector
        def _(dve):
            chain = Chain(dve, vch)
            for t in range(NT + 1):
                if t < NT:
                    dve.wait_ge(sq, t + 1)
                    chain(nc.vector.tensor_scalar(rs[:, t % 2], ss[:, t % 2], 1.0 / D, RMS_EPS, ALU.mult, ALU.add))
                    rsqrt(nc, chain, rs[:, t % 2], ri[:, t % 2], rt)
                    if t >= 2:
                        dve.wait_ge(turned, t - 1)
                    nc.vector.tensor_scalar(XN[:, t % 2], X[:, t % 2], ri[:, t % 2], None,
                                            ALU.mult).then_inc(xn_ready, 1)
                if t >= 1:
                    u = t - 1
                    j = 1 if u < CT else 0
                    dve.wait_ge(turned, u + 1)
                    for c in range(KC // 2, KC):
                        nc.vector.tensor_scalar(k.hT[:, c, u * P:(u + 1) * P],
                                                k.ps[4 * (u % 2) + c // 4][:, (c % 4) * P:(c % 4 + 1) * P],
                                                k.mul_col[0][j][:, c:c + 1], k.add_col[0][j][:, c:c + 1],
                                                ALU.mult, ALU.add).then_inc(out[1], 1)

        @block.tensor
        def _(pe):
            for t in range(NT):
                pe.wait_ge(xn_ready, t + 1)
                if t >= 2:
                    for o in out:
                        pe.wait_ge(o, KC // 2 * (t - 1))
                for c in range(KC):
                    last = nc.tensor.transpose(k.ps[4 * (t % 2) + c // 4][:, (c % 4) * P:(c % 4 + 1) * P],
                                               XN[:, t % 2, c::KC], k.ident)
                last.then_inc(turned, 1)


def project(nc, k, ctx, cr, w_in, name, groups):
    sem = lambda n: ctx.semaphore(name + n)
    w_ready = [sem("_w_even_loaded"), sem("_w_odd_loaded")]
    used, done = sem("_w_used"), sem("_product_done")
    out = [sem("_even_product_out"), sem("_odd_product_out")]
    W = cr.take(2, KC, 512)
    view = w_in[0].rearrange("(p c) n -> p c n", c=KC)

    def products(width, dest, by_token):
        if by_token:
            for t in range(NT):
                yield slice(t * P, (t + 1) * P), slice(0, width), P, width, dest[:, t, :]
        else:
            for m in range(0, width, P):
                rows = min(P, width - m)
                for a in range(0, TOK, 512):
                    n = min(512, TOK - a)
                    to = dest[:, m // P, a:a + n] if width > P else dest[0:rows, a:a + n]
                    yield slice(a, a + n), slice(m, m + rows), rows, n, to

    with nc.Block() as block:
        @block.sync
        def _(sp):
            for g, (at, width, dest, by_token) in enumerate(groups):
                if g >= 2:
                    sp.wait_ge(used, g - 1)
                sp.dma_start(W[:, g % 2, :, 0:width], view[:, :, at:at + width]).then_inc(w_ready[g % 2], 16)

        @block.tensor
        def _(pe):
            n = 0
            for g, (at, width, dest, by_token) in enumerate(groups):
                pe.wait_ge(w_ready[g % 2], 16 * (g // 2 + 1))
                for toks, ws, rows, cols, _dst in products(width, dest, by_token):
                    if n >= 4:
                        pe.wait_ge(out[n % 2], (n - 4) // 2 + 1)
                    for c in range(KC):
                        h, w = k.hT[:, c, toks], W[:, g % 2, c, ws]
                        last = nc.tensor.matmul(k.ps[n % 4][0:rows, 0:cols], h if by_token else w,
                                                w if by_token else h, start=(c == 0), stop=(c == KC - 1))
                    last.then_inc(done, 1)
                    n += 1
                pe.wait_ge(done, n)
                pe.sem_inc(used, 1)

        def leave(eng, copy, parity):
            n = 0
            for at, width, dest, by_token in groups:
                for _toks, _ws, rows, cols, dst in products(width, dest, by_token):
                    if n % 2 == parity:
                        eng.wait_ge(done, n + 1)
                        copy(dst, k.ps[n % 4][0:rows, 0:cols]).then_inc(out[parity], 1)
                    n += 1

        @block.scalar
        def _(act):
            leave(act, nc.scalar.copy, 0)

        @block.vector
        def _(dve):
            leave(dve, nc.vector.tensor_copy, 1)


def write_out(sp, y, y_dram, m, written):
    sp.dma_start(y_dram[:, m * GW:(m + 1) * GW].rearrange("(t p) n -> p t n", p=P), y).then_inc(written, 16)
    sp.wait_ge(written, 16)


def gla(nc, k, ctx, cr, w_in, gate_w2, gate_b, norm_g, y_dram):
    sem = lambda n: ctx.semaphore("gla_" + n)
    QKVG = cr.take(NT, 4 * GW)
    LS = cr.take(NT, 2 * GW)
    DEC = cr.take(2, NT, 2, 2)
    O = cr.take(2, NT, GW)
    top = cr.at
    glT = cr.take(TOK)
    W2 = cr.take(2 * GW)
    project(nc, k, ctx, Carve(cr.arena, cr.at), w_in, "gla", [
        (A_Q, 512, QKVG[:, :, 0:512], True), (A_Q + 512, 512, QKVG[:, :, 512:1024], True),
        (A_GL, 32, glT, False)])

    w2_in, w2_zero, z_ready, ln, ls, ach = (sem("w2_loaded"), sem("w2_zeroed"), sem("z_ready"), sem("log1p_ready"),
                                            sem("log_sigmoid_ready"), sem("act_chain"))
    dec_ready, dec_out = sem("decay_sums"), sem("decays")
    with nc.Block() as block:
        @block.vector
        def _(dve):
            nc.vector.memset(W2[0:32, :], 0.0).then_inc(w2_zero, 1)
            nc.vector.memset(glT[32:33, :], 1.0).then_inc(w2_zero, 1)
            for t in range(NT):
                dve.wait_ge(ln, t + 1)
                nc.vector.scalar_tensor_tensor(LS[:, t, :], k.ps[t % 4][:, 0:512], 0.0, LS[:, t, :],
                                               ALU.min, ALU.subtract).then_inc(ls, 1)

        @block.sync
        def _(sp):
            sp.wait_ge(w2_zero, 2)
            for d in range(2):
                sp.dma_start(W2[16 * d:16 * d + 16, d * GW:(d + 1) * GW], gate_w2[0, d]).then_inc(w2_in, 16)
            sp.dma_start(W2[32:33, :], gate_b.rearrange("a d n -> a (d n)")).then_inc(w2_in, 16)

        @block.tensor
        def _(pe):
            pe.wait_ge(w2_in, 48)
            for t in range(NT):
                if t >= 4:
                    pe.wait_ge(ls, t - 3)
                nc.tensor.matmul(k.ps[t % 4][:, 0:512], glT[0:33, t * P:(t + 1) * P], W2[0:33, :],
                                 start=True, stop=True).then_inc(z_ready, 1)
            pe.wait_ge(ls, NT)
            for d in range(2):
                for t in range(NT):
                    for p in range(2):
                        at = ((d * NT + t) * 2 + p) * 2
                        last = nc.tensor.matmul(k.ps[4][:, at:at + 2], LS[:, t, d * GW + p * P:d * GW + (p + 1) * P],
                                                k.blk[64][:, 0:P:64], start=True, stop=True)
            last.then_inc(dec_ready, 1)

        @block.scalar
        def _(act):
            chain = Chain(act, ach)
            for t in range(NT):
                act.wait_ge(z_ready, t + 1)
                chain(nc.scalar.activation(LS[:, t, :], k.ps[t % 4][:, 0:512], ACT.Abs))
                chain(nc.scalar.activation(LS[:, t, :], LS[:, t, :], ACT.Exp, scale=-1.0))
                nc.scalar.activation(LS[:, t, :], LS[:, t, :], ACT.Ln, bias=1.0).then_inc(ln, 1)
            act.wait_ge(dec_ready, 1)
            nc.scalar.activation(DEC.rearrange("p d t s q -> p d t q s"), k.ps[4][:, 0:2 * NT * 4].rearrange(
                "p (d t q s) -> p d t q s", d=2, t=NT, q=2), ACT.Exp, scale=1.0 / 16.0).then_inc(dec_out, 1)
            act.wait_ge(dec_out, 1)

    cr = Carve(cr.arena, top)
    EB, ENB, QK, V, ATT = (cr.take(2, GW), cr.take(2, GW), cr.take(2, 2 * GW), cr.take(2, GW), cr.take(2, NH, P))
    KT = cr.take(2, 2, P)
    QT = cr.take(2, NH, P)
    S, SM, UL, tmp = (cr.take(2, 2, HD) for _ in range(4))
    pe_s, act_s, dve_s, vch = sem("pe_stage"), sem("act_stage"), sem("dve_stage"), sem("dve_chain")
    qt_zero = sem("q_zeroed")
    CUM, TURN, SCORE, OUT, NPE = 0, 1, 2, 3, 4
    EXPS, TURNED, NACT = 0, 1, 2
    SCALED, MASKED, CLOSED, NDVE = 0, 1, 2, 3
    at = lambda i, stage, d, n: i * (2 * n) + (2 * stage + d + 1)
    tile = lambda i, d: i if d == 0 else (NT + 1 - i) % NT
    pb = [k.ps[3 * d][:, 0:GW] for d in range(2)]
    pu = [[k.ps[3 * d + c][:, (1 - c) * GW:(1 - c) * GW + P].rearrange("p (q v) -> p q v", q=2) for c in range(2)]
          for d in range(2)]
    pt = [k.ps[3 * d + 1] for d in range(2)]
    pa = [k.ps[3 * d + 2] for d in range(2)]
    po = [k.ps[6 + d][:, 0:GW] for d in range(2)]
    ps = [k.ps[6 + d][:, GW:2 * GW] for d in range(2)]
    with nc.Block() as block:
        @block.tensor
        def _(pe):
            with pe.Fori(0, NT) as i:
                for d in range(2):
                    nc.tensor.matmul(pb[d], k.glacum[d], LS[:, tile(i, d), d * GW:(d + 1) * GW],
                                     start=True, stop=True).then_inc(pe_s, 1)
                for d in range(2):
                    hold(pe, dve_s, at(i, SCALED, d, NDVE))
                    for n in range(4):
                        last = nc.tensor.transpose(pt[d][:, n * P:(n + 1) * P], QK[:, d, n * P:(n + 1) * P], k.ident)
                    last.then_inc(pe_s, 1)
                for d in range(2):
                    hold(pe, act_s, at(i, TURNED, d, NACT))
                    for h in range(NH):
                        nc.tensor.matmul(pa[d][:, h * P:(h + 1) * P], KT[:, d, h // 2, :], QT[:, d, h, :],
                                         start=True, stop=True)
                    for c in range(2):
                        j = slice(64 * c, 64 * c + 64)
                        for h in range(NH):
                            r = slice(HD * (h % 2), HD * (h % 2) + HD)
                            last = nc.tensor.matmul(pu[d][c][r, h // 2, :], QK[j, d, GW + h * HD:GW + (h + 1) * HD],
                                                    V[j, d, h * HD:(h + 1) * HD], start=True, stop=True)
                    last.then_inc(pe_s, 1)
                for d in range(2):
                    hold(pe, dve_s, at(i, MASKED, d, NDVE))
                    for h in range(NH):
                        nc.tensor.matmul(po[d][:, h * HD:(h + 1) * HD], ATT[:, d, h, :], V[:, d, h * HD:(h + 1) * HD],
                                         start=True, stop=True)
                    for c in range(2):
                        j = slice(64 * c, 64 * c + 64)
                        state = S if c == d else SM
                        for h in range(NH):
                            last = nc.tensor.matmul(ps[d][j, h * HD:(h + 1) * HD], QT[:, d, h, j],
                                                    state[:, d, h // 2, :], start=True, stop=True)
                    last.then_inc(pe_s, 1)

        @block.scalar
        def _(act):
            act.wait_ge(qt_zero, 1)
            with act.Fori(0, NT) as i:
                for d in range(2):
                    hold(act, pe_s, at(i, CUM, d, NPE))
                    nc.scalar.activation(EB[:, d], pb[d], ACT.Exp)
                    nc.scalar.activation(ENB[:, d], pb[d], ACT.Exp, scale=-1.0).then_inc(act_s, 1)
                for d in range(2):
                    hold(act, pe_s, at(i, TURN, d, NPE))
                    turned = pt[d].rearrange("p (n m) -> p n m", n=4)
                    nc.scalar.copy(KT[:, d], turned[:, 2:4])
                    nc.scalar.copy(QT[0:HD, d, 0::2], turned[0:HD, 0:2])
                    nc.scalar.copy(QT[HD:P, d, 1::2], turned[HD:P, 0:2]).then_inc(act_s, 1)

        @block.vector
        def _(dve):
            chain = Chain(dve, vch)
            chain(nc.vector.memset(S, 0.0))
            nc.vector.memset(QT, 0.0).then_inc(qt_zero, 1)
            with dve.Fori(0, NT) as i:
                chain.enter(i, 6)
                for d in range(2):
                    x = lambda n: QKVG[:, tile(i, d), n * GW:(n + 1) * GW]
                    hold(dve, act_s, at(i, EXPS, d, NACT))
                    nc.vector.scalar_tensor_tensor(QK[:, d, 0:GW], x(0), HD ** -0.5, EB[:, d], ALU.mult, ALU.mult)
                    nc.vector.tensor_tensor(QK[:, d, GW:2 * GW], x(1), ENB[:, d], ALU.mult)
                    nc.vector.tensor_copy(V[:, d], x(2)).then_inc(dve_s, 1)
                for d in range(2):
                    hold(dve, pe_s, at(i, SCORE, d, NPE))
                    first = d
                    chain(nc.vector.tensor_tensor(tmp[:, d], S[:, d], pu[d][first], ALU.add))
                    nc.vector.tensor_tensor(SM[:, d], tmp[:, d], over(DEC[:, d, tile(i, d), first, :], HD), ALU.mult)
                    nc.vector.tensor_copy(UL[:, d], pu[d][1 - first])
                    nc.vector.tensor_tensor(ATT[:, d], pa[d].rearrange("p (h n) -> p h n", h=NH),
                                            each(k.glamask[d], NH), ALU.mult).then_inc(dve_s, 1)
                for d in range(2):
                    hold(dve, pe_s, at(i, OUT, d, NPE))
                    hold(dve, dve_s, at(i, MASKED, d, NDVE))
                    chain(nc.vector.tensor_copy(O[:, d, tile(i, d), :], po[d]))
                    nc.vector.tensor_tensor(O[:, d, tile(i, d), :], O[:, d, tile(i, d), :],
                                            ps[d], ALU.add)
                    chain(nc.vector.tensor_tensor(tmp[:, d], SM[:, d], UL[:, d], ALU.add))
                    nc.vector.tensor_tensor(S[:, d], tmp[:, d], over(DEC[:, d, tile(i, d), 1 - d, :], HD),
                                            ALU.mult).then_inc(dve_s, 1)
                hold(dve, dve_s, at(i, CLOSED, 1, NDVE))
                chain.leave(NT)

    head_norm_gate(nc, k, ctx, Carve(cr.arena, top), "gla", O, QKVG[:, CT:, 3 * GW:4 * GW], norm_g, y_dram, 0)


def head_norm_gate(nc, k, ctx, cr, name, O, G, norm_g, y_dram, m):
    sem = lambda n: ctx.semaphore(name + "_post_" + n)
    gain_in, silu, ready, written, vch = sem("gain_loaded"), sem("silu"), sem("ready"), sem("written"), sem("chain")
    gain = cr.take(GW)
    SQ = cr.take(XT, GW)
    GS = cr.take(XT, GW)
    Y = cr.take(XT, GW)
    ss, rs, rt = (cr.take(XT * NH) for _ in range(3))
    hv = lambda ap: ap.rearrange("p t (h d) -> p (t h) d", h=NH)
    with nc.Block() as block:
        @block.sync
        def _(sp):
            sp.dma_start(gain, norm_g[0:1, :].to_broadcast([P, GW])).then_inc(gain_in, 16)
            sp.wait_ge(ready, 1)
            write_out(sp, Y, y_dram, m, written)

        @block.scalar
        def _(act):
            nc.scalar.activation(GS, G, ACT.Silu).then_inc(silu, 1)

        @block.vector
        def _(dve):
            chain = Chain(dve, vch)
            chain(nc.vector.tensor_tensor(Y, O[:, 0, CT:, :], O[:, 1, CT:, :], ALU.add))
            chain(nc.vector.tensor_tensor(SQ, Y, Y, ALU.mult))
            chain(nc.vector.tensor_reduce(ss, hv(SQ), AX.X, ALU.add))
            chain(nc.vector.tensor_scalar(ss, ss, 1.0 / HD, RMS_EPS, ALU.mult, ALU.add))
            rsqrt(nc, chain, ss, rs, rt)
            chain(nc.vector.tensor_tensor(hv(Y), hv(Y), over(rs, HD), ALU.mult))
            dve.wait_ge(gain_in, 16)
            chain(nc.vector.tensor_tensor(Y, Y, each(gain, XT), ALU.mult))
            dve.wait_ge(silu, 1)
            nc.vector.tensor_tensor(Y, Y, GS, ALU.mult).then_inc(ready, 1)


def conv_silu(nc, k, ctx, cr, name, U, C, T, conv_w, conv_b, turned):
    sem = lambda n: ctx.semaphore(name + "_conv_" + n)
    w_in, w_turned, w_out, acc, silu, tr = (sem("w_loaded"), sem("w_turned"), sem("w_ready"), sem("sum_done"),
                                            sem("silu_done"), sem("token_tile_ready"))
    out = [sem("token_tile_out_by_act"), sem("token_tile_out_by_dve")]
    vch = sem("chain")
    n_ct = U.shape[1]
    rows = 9 * n_ct + (n_ct if conv_b is not None else 0)
    WR = cr.take(P)
    WC = cr.take(rows)
    per = 4 if len(turned) == 4 else 3
    jobs = [(t, a) for t in range(NT) for a in range(0, len(turned), per)]
    with nc.Block() as block:
        @block.sync
        def _(sp):
            sp.dma_start(WR[0:9 * n_ct, :], conv_w.rearrange("a kh kw (ct p) -> (a kh kw ct) p", p=P)).then_inc(w_in, 16)
            if conv_b is not None:
                sp.dma_start(WR[9 * n_ct:rows, :], conv_b.rearrange("a (ct p) -> (a ct) p", p=P)).then_inc(w_in, 16)

        @block.tensor
        def _(pe):
            pe.wait_ge(w_in, 16 if conv_b is None else 32)
            nc.tensor.transpose(k.ps[0][:, 0:rows], WR[0:rows, :], k.ident[0:rows, 0:rows]).then_inc(w_turned, 1)
            pe.wait_ge(w_out, 1)
            pe.wait_ge(silu, n_ct)
            for n, (t, a) in enumerate(jobs):
                if n >= 8:
                    pe.wait_ge(out[n % 2], (n - 8) // 2 + 1)
                for m, ct in enumerate(turned[a:a + per]):
                    last = nc.tensor.transpose(k.ps[n % 8][:, m * P:(m + 1) * P], C[:, ct, t * P:(t + 1) * P], k.ident)
                last.then_inc(tr, 1)

        def leave(eng, copy, parity):
            for n, (t, a) in enumerate(jobs):
                if n % 2 == parity:
                    eng.wait_ge(tr, n + 1)
                    w = min(per, len(turned) - a) * P
                    copy(T[:, t, a * P:a * P + w], k.ps[n % 8][:, 0:w]).then_inc(out[parity], 1)

        @block.vector
        def _(dve):
            chain = Chain(dve, vch)
            dve.wait_ge(w_turned, 1)
            nc.vector.tensor_copy(WC, k.ps[0][:, 0:rows]).then_inc(w_out, 1)
            dve.wait_ge(w_out, 1)
            grid = lambda buf, ct: buf[:, ct, CTX:].rearrange("p (r c) -> p r c", c=GRID)
            for pair in range(0, n_ct, 2):
                cts = (pair, pair + 1)
                for ct in cts:
                    last = nc.vector.tensor_scalar(C[:, ct, :], U[:, ct, :], WC[:, 4 * n_ct + ct:4 * n_ct + ct + 1],
                                                   None, ALU.mult)
                chain(last)
                for tap in (0, 1, 2, 3, 5, 6, 7, 8):
                    dr, dc = tap // 3 - 1, tap % 3 - 1
                    r0, r1 = max(0, -dr), ROWS - max(0, dr)
                    c0, c1 = max(0, -dc), GRID - max(0, dc)
                    for ct in cts:
                        w = WC[:, tap * n_ct + ct:tap * n_ct + ct + 1]
                        o = grid(C, ct)[:, r0:r1, c0:c1]
                        last = nc.vector.scalar_tensor_tensor(o, grid(U, ct)[:, r0 + dr:r1 + dr, c0 + dc:c1 + dc],
                                                              w, o, ALU.mult, ALU.add)
                        if dr == 0:
                            a, b = max(0, -dc), CTX - max(0, dc)
                            o = C[:, ct, a:b]
                            last = nc.vector.scalar_tensor_tensor(o, U[:, ct, a + dc:b + dc], w, o, ALU.mult, ALU.add)
                    if tap < 8:
                        chain(last)
                    else:
                        last.then_inc(acc, 1)
            leave(dve, nc.vector.tensor_copy, 1)

        @block.scalar
        def _(act):
            for ct in range(n_ct):
                act.wait_ge(acc, ct // 2 + 1)
                bias = 0.0 if conv_b is None else WC[:, 9 * n_ct + ct:9 * n_ct + ct + 1]
                nc.scalar.activation(C[:, ct, :], C[:, ct, :], ACT.Silu, bias=bias).then_inc(silu, 1)
            leave(act, nc.scalar.copy, 0)


def decay_rates(nc, k, ctx, cr, name, raw, dt_bias, a_log, DT, A, beta_raw, BETA):
    sem = lambda n: ctx.semaphore(name + "_rate_" + n)
    par_in, v_ready, ea, ex, w_ready, ln, vch = (sem("loaded"), sem("abs_ready"), sem("exp_a_ready"),
                                                 sem("exp_ready"), sem("one_plus_ready"), sem("ln_ready"), sem("chain"))
    n = NT * 2 * NH
    bias, al = cr.take(2 * NH), cr.take(2 * NH)
    v, u, w, l, s = (cr.take(NT, 2 * NH) for _ in range(5))
    with nc.Block() as block:
        @block.sync
        def _(sp):
            sp.dma_start(bias, dt_bias.rearrange("a d h -> a (d h)").to_broadcast([P, 2 * NH])).then_inc(par_in, 16)
            sp.dma_start(al, a_log.rearrange("a d h -> a (d h)").to_broadcast([P, 2 * NH])).then_inc(par_in, 16)

        @block.scalar
        def _(act):
            act.wait_ge(par_in, 32)
            nc.scalar.activation(al, al, ACT.Exp).then_inc(ea, 1)
            act.wait_ge(v_ready, 1)
            if BETA is not None:
                nc.scalar.activation(BETA, beta_raw, ACT.Exp, scale=-1.0)
            nc.scalar.activation(u, u, ACT.Exp, scale=-1.0).then_inc(ex, 1)
            act.wait_ge(w_ready, 1)
            nc.scalar.activation(l, w, ACT.Ln).then_inc(ln, 1)

        @block.vector
        def _(dve):
            chain = Chain(dve, vch)
            dve.wait_ge(par_in, 32)
            chain(nc.vector.tensor_tensor(v, raw, each(bias, NT), ALU.add))
            chain(nc.vector.tensor_scalar(s, v, -1.0, None, ALU.mult))
            nc.vector.tensor_tensor(u, v, s, ALU.max).then_inc(v_ready, 1)
            dve.wait_ge(ex, 1)
            nc.vector.tensor_scalar(w, u, 1.0, None, ALU.add).then_inc(w_ready, 1)
            dve.wait_ge(w_ready, 1)
            chain(nc.vector.tensor_scalar(s, w, 1.0, None, ALU.subtract))
            chain(nc.vector.tensor_tensor(s, u, s, ALU.subtract))
            chain(nc.vector.scalar_tensor_tensor(s, v, 0.0, s, ALU.max, ALU.add))
            dve.wait_ge(ln, 1)
            chain(nc.vector.tensor_tensor(DT, s, l, ALU.add))
            dve.wait_ge(ea, 1)
            chain(nc.vector.scalar_tensor_tensor(A, DT, -1.0, each(al, NT), ALU.mult, ALU.mult))
            if BETA is not None:
                chain(nc.vector.tensor_scalar(BETA, BETA, 1.0, None, ALU.add))
                chain(nc.vector.reciprocal(BETA, BETA))


def mamba(nc, k, ctx, cr, w_in, conv_w, conv_b, a_log, dt_bias, d_skip, norm_g, y_dram):
    sem = lambda n: ctx.semaphore("ssm_" + n)
    C = cr.take(6, TOK)
    T = cr.take(NT, 4 * P)
    Z = cr.take(NT, GW)
    RAW, DT, A = (cr.take(NT, 2 * NH) for _ in range(3))
    top = cr.at
    U = cr.take(6, TOK)
    project(nc, k, ctx, Carve(cr.arena, cr.at), w_in, "ssm", [
        (C_Z, GW, Z, True), (C_XBC, 384, U[:, 0:3], False), (C_XBC + 384, 384, U[:, 3:6], False),
        (C_DT, 2 * NH, RAW, True)])
    conv_silu(nc, k, ctx, Carve(cr.arena, cr.at), "ssm", U, C, T, conv_w, conv_b, (0, 1, 2, 3))
    cr = Carve(cr.arena, top)
    decay_rates(nc, k, ctx, Carve(cr.arena, cr.at), "ssm", RAW, dt_bias, a_log, DT, A, None, None)

    O = cr.take(2, NT, GW)
    top = cr.at
    AC, SM, EX = cr.take(2, NH), cr.take(2, 3 * NH), cr.take(2, 3 * NH)
    LT, MT, XD, XE, BC, BT, CTc = (cr.take(2, NH, P), cr.take(2, NH, P), cr.take(2, GW), cr.take(2, GW),
                                   cr.take(2, GW), cr.take(2, 2, P), cr.take(2, 2, P))
    S, tmp, tmp2 = cr.take(2, GW), cr.take(2, GW), cr.take(2, GW)
    pe_s, act_s, dve_s, vch = sem("pe_stage"), sem("act_stage"), sem("dve_stage"), sem("dve_chain")
    SUMS, OUT, NPE = 0, 1, 2
    COPIED, EXPS, NACT = 0, 1, 2
    LOAD, CAPS, MIX, CLOSE, NDVE = 0, 1, 2, 3, 4
    at = lambda i, stage, d, n: i * (2 * n) + (2 * stage + d + 1)
    tile = lambda i, d: i if d == 0 else (NT + 1 - i) % NT
    bank = lambda d, n: k.ps[3 * d + n]
    hv = heads
    with nc.Block() as block:
        @block.tensor
        def _(pe):
            with pe.Fori(0, NT) as i:
                for d in range(2):
                    hold(pe, dve_s, at(i, LOAD, d, NDVE))
                    hold(pe, act_s, at(i, COPIED, d, NACT))
                    for h in range(NH):
                        nc.tensor.matmul(bank(d, 0)[:, h * P:(h + 1) * P], AC[:, d, h:h + 1].to_broadcast([P, P]),
                                         k.incl[d], start=True, stop=True)
                    nc.tensor.matmul(bank(d, 1)[:, 0:NH], k.incl[d], AC[:, d], start=True, stop=True)
                    nc.tensor.matmul(bank(d, 1)[:, NH:2 * NH], k.ones, AC[:, d], start=True, stop=True)
                    for g in range(2):
                        last = nc.tensor.matmul(bank(d, 2)[:, g * P:(g + 1) * P], BT[:, d, g], CTc[:, d, g],
                                                start=True, stop=True)
                    last.then_inc(pe_s, 1)
                for d in range(2):
                    hold(pe, dve_s, at(i, MIX, d, NDVE))
                    for h in range(NH):
                        c = slice(h * HD, (h + 1) * HD)
                        nc.tensor.matmul(bank(d, 0)[:, c], MT[:, d, h], XD[:, d, c], start=True, stop=True)
                    for g in range(2):
                        c = slice(g * P, (g + 1) * P)
                        nc.tensor.matmul(bank(d, 0)[:, GW + g * P:GW + (g + 1) * P], BC[:, d, c], XE[:, d, c],
                                         start=True, stop=True)
                        last = nc.tensor.matmul(bank(d, 1)[:, GW + g * P:GW + (g + 1) * P], CTc[:, d, g], S[:, d, c],
                                                start=True, stop=True)
                    last.then_inc(pe_s, 1)

        @block.scalar
        def _(act):
            with act.Fori(0, NT) as i:
                for d in range(2):
                    hold(act, dve_s, at(i, LOAD, d, NDVE))
                    nc.scalar.copy(BT[:, d], C[:, 2:4, bass.ds(tile(i, d) * P, P)])
                    nc.scalar.copy(CTc[:, d], C[:, 4:6, bass.ds(tile(i, d) * P, P)]).then_inc(act_s, 1)
                for d in range(2):
                    hold(act, dve_s, at(i, CAPS, d, NDVE))
                    nc.scalar.activation(LT[:, d], LT[:, d], ACT.Exp)
                    nc.scalar.activation(EX[:, d], SM[:, d], ACT.Exp).then_inc(act_s, 1)

        @block.vector
        def _(dve):
            chain = Chain(dve, vch)
            chain(nc.vector.memset(S, 0.0))
            with dve.Fori(0, NT) as i:
                chain.enter(i, 4)
                for d in range(2):
                    t = tile(i, d)
                    r = slice(d * NH, (d + 1) * NH)
                    nc.vector.tensor_copy(AC[:, d], A[:, t, r])
                    nc.vector.tensor_tensor(hv(XD[:, d]), hv(T[:, t, 0:GW]), over(DT[:, t, r], HD), ALU.mult)
                    nc.vector.tensor_copy(BC[:, d], T[:, t, GW:2 * GW]).then_inc(dve_s, 1)
                for d in range(2):
                    hold(dve, pe_s, at(i, SUMS, d, NPE))
                    nc.vector.tensor_copy(SM[:, d, 0:NH], bank(d, 1)[:, 0:NH])
                    chain(nc.vector.tensor_copy(SM[:, d, 2 * NH:], bank(d, 1)[:, NH:2 * NH]))
                    nc.vector.tensor_tensor(SM[:, d, NH:2 * NH], SM[:, d, 2 * NH:], SM[:, d, 0:NH], ALU.subtract)
                    for h in range(NH):
                        last = nc.vector.scalar_tensor_tensor(LT[:, d, h], bank(d, 0)[:, h * P:(h + 1) * P],
                                                              SM[:, d, h:h + 1], k.cap[d], ALU.subtract, ALU.min)
                    last.then_inc(dve_s, 1)
                for d in range(2):
                    hold(dve, act_s, at(i, EXPS, d, NACT))
                    nc.vector.tensor_tensor(MT[:, d].rearrange("p (g q) n -> p g q n", g=2),
                                            LT[:, d].rearrange("p (g q) n -> p g q n", g=2),
                                            bank(d, 2)[:, 0:GW].rearrange("p (g n) -> p g n", g=2).unsqueeze(
                                                2).to_broadcast([P, 2, 2, P]), ALU.mult)
                    nc.vector.tensor_tensor(hv(XE[:, d]), hv(XD[:, d]), over(EX[:, d, NH:2 * NH], HD),
                                            ALU.mult).then_inc(dve_s, 1)
                for d in range(2):
                    hold(dve, pe_s, at(i, OUT, d, NPE))
                    nc.vector.tensor_tensor(hv(tmp[:, d]), hv(bank(d, 1)[:, GW:2 * GW]), over(EX[:, d, 0:NH], HD),
                                            ALU.mult)
                    chain(nc.vector.tensor_tensor(hv(tmp2[:, d]), hv(S[:, d]), over(EX[:, d, 2 * NH:], HD), ALU.mult))
                    nc.vector.tensor_tensor(O[:, d, tile(i, d), :], tmp[:, d], bank(d, 0)[:, 0:GW], ALU.add)
                    nc.vector.tensor_tensor(S[:, d], tmp2[:, d], bank(d, 0)[:, GW:2 * GW], ALU.add).then_inc(dve_s, 1)
                hold(dve, dve_s, at(i, CLOSE, 1, NDVE))
                chain.leave(NT)

    cr = Carve(cr.arena, top)
    par_in, silu, ready, written, vch2 = (sem("post_loaded"), sem("post_silu"), sem("post_ready"), sem("post_written"),
                                          sem("post_chain"))
    gain, dsk = cr.take(GW), cr.take(NH)
    Y, SQ, GS = (cr.take(XT, GW) for _ in range(3))
    ss, rs, rt = (cr.take(XT * 2) for _ in range(3))
    with nc.Block() as block:
        @block.sync
        def _(sp):
            sp.dma_start(gain, norm_g[0:1, :].to_broadcast([P, GW])).then_inc(par_in, 16)
            sp.dma_start(dsk, d_skip[0:1, :].to_broadcast([P, NH])).then_inc(par_in, 16)
            sp.wait_ge(ready, 1)
            write_out(sp, Y, y_dram, 2, written)

        @block.scalar
        def _(act):
            nc.scalar.activation(GS, Z[:, CT:, :], ACT.Silu).then_inc(silu, 1)

        @block.vector
        def _(dve):
            chain = Chain(dve, vch2)
            dve.wait_ge(par_in, 32)
            for h in range(NH):
                c = slice(h * HD, (h + 1) * HD)
                last = nc.vector.scalar_tensor_tensor(Y[:, :, c], T[:, CT:, c], dsk[:, h:h + 1], O[:, 0, CT:, c],
                                                      ALU.mult, ALU.add)
            chain(last)
            chain(nc.vector.tensor_tensor(Y, Y, O[:, 1, CT:, :], ALU.add))
            dve.wait_ge(silu, 1)
            chain(nc.vector.tensor_tensor(Y, Y, GS, ALU.mult))
            chain(nc.vector.tensor_tensor(SQ, Y, Y, ALU.mult))
            groups = lambda b: b.rearrange("p t (g n) -> p (t g) n", g=2)
            chain(nc.vector.tensor_reduce(ss, groups(SQ), AX.X, ALU.add))
            chain(nc.vector.tensor_scalar(ss, ss, 1.0 / P, RMS_EPS, ALU.mult, ALU.add))
            rsqrt(nc, chain, ss, rs, rt)
            chain(nc.vector.tensor_tensor(groups(Y), groups(Y), over(rs, P), ALU.mult))
            nc.vector.tensor_tensor(Y, Y, each(gain, XT), ALU.mult).then_inc(ready, 1)


class Inverse:

    NPE, NACT, NDVE = 10, 6, 7
    LINKS = 0

    def __init__(self, nc, k, sem, cr, banks):
        self.nc, self.k, self.b = nc, k, banks
        self.D, self.DT, self.Y, self.X, self.T1, self.N = (cr.take(2, NH, P) for _ in range(6))
        self.NL = {b: cr.take(2, NH, P) for b in (32, 64, 128)}
        self.pe_s, self.act_s, self.dve_s, self.pool_s = (sem("inv_pe_stage"), sem("inv_act_stage"),
                                                         sem("inv_dve_stage"), sem("inv_pool_stage"))

    @staticmethod
    def at(i, stage, d, n):
        return i * (2 * n) + (2 * stage + d + 1)

    def solved(self, eng, i, d):
        hold(eng, self.dve_s, self.at(i, 6, d, self.NDVE))

    def products(self, d, bank, lhsT, rhs):
        for h in range(NH):
            last = self.nc.tensor.matmul(self.b(d, bank)[:, h * P:(h + 1) * P], lhsT[:, d, h], rhs[:, d, h],
                                         start=True, stop=True)
        return last

    def tensor(self, pe, i, ready_sem, ready_at):
        at, prod = self.at, self.products
        for stage, a, v, what in (
                (0, None, None, ((0, self.DT, self.D), (1, self.D, self.DT))),
                (1, 0, 0, ((0, self.DT, self.D), (1, self.D, self.DT), (2, self.D, self.Y))),
                (2, 1, 1, ((0, self.DT, self.D), (2, self.D, self.Y))),
                (3, 2, 2, ((2, self.D, self.Y),)),
                (4, None, 3, None),
                (5, 3, None, ((2, self.X, self.T1), (0, self.T1, self.X))),
                (6, None, 4, ((1, self.NL[64], self.Y),)),
                (7, 4, None, ((2, self.X, self.T1), (0, self.T1, self.X))),
                (8, None, 5, ((1, self.NL[128], self.Y),)),
                (9, 5, None, ((2, self.X, self.T1),))):
            for d in range(2):
                if stage == 0:
                    hold(pe, ready_sem, ready_at(d))
                if stage == 4:
                    hold(pe, self.pool_s, at(i, 0, d, 1))
                if a is not None:
                    hold(pe, self.act_s, at(i, a, d, self.NACT))
                if v is not None:
                    hold(pe, self.dve_s, at(i, v, d, self.NDVE))
                if stage == 4:
                    for h in range(NH):
                        self.nc.tensor.transpose(self.b(d, 0)[:, h * P:(h + 1) * P], self.Y[:, d, h], self.k.ident)
                    last = prod(d, 1, self.NL[32], self.Y)
                else:
                    for bank, lhsT, rhs in what:
                        last = prod(d, bank, lhsT, rhs)
                last.then_inc(self.pe_s, 1)

    def scalar(self, act, i):
        bank = lambda d, n: heads(self.b(d, n)[:, :])
        for after, what in ((0, ((self.D, 0),)), (1, ((self.D, 0),)), (2, ((self.D, 0),)),
                            (4, ((self.X, 0), (self.T1, 1))), (6, ((self.T1, 1),)), (8, ((self.T1, 1),))):
            for d in range(2):
                hold(act, self.pe_s, self.at(i, after, d, self.NPE))
                for dst, n in what:
                    last = self.nc.scalar.copy(dst[:, d], bank(d, n))
                last.then_inc(self.act_s, 1)

    def vector(self, dve, i):
        bank = lambda d, n: heads(self.b(d, n)[:, :])
        for after, what in ((0, ("DT",)), (1, ("DT", "Y")), (2, ("Y",)), (3, ("Y",)), (5, ("Y", "X")),
                            (7, ("Y", "X")), (9, ("Y",))):
            for d in range(2):
                hold(dve, self.pe_s, self.at(i, after, d, self.NPE))
                for name in what:
                    if name == "DT":
                        last = self.nc.vector.tensor_copy(self.DT[:, d], bank(d, 1))
                    elif name == "Y":
                        last = self.nc.vector.tensor_tensor(self.Y[:, d], self.Y[:, d], bank(d, 2), ALU.add)
                    else:
                        last = self.nc.vector.tensor_tensor(self.X[:, d], self.X[:, d], bank(d, 0), ALU.add)
                last.then_inc(self.dve_s, 1)

    def pool(self, pool, i, ready_sem, ready_at):
        for d in range(2):
            hold(pool, ready_sem, ready_at(d))
            for b in (32, 64, 128):
                last = self.nc.gpsimd.tensor_tensor(self.NL[b][:, d], self.N[:, d], each(self.k.lvl[b], NH), ALU.mult)
            last.then_inc(self.pool_s, 1)


def deltanet(nc, k, ctx, cr, w_in, conv_w, a_log, dt_bias, norm_g, y_dram):
    sem = lambda n: ctx.semaphore("dn_" + n)
    T = cr.take(NT, 3 * GW)
    Z = cr.take(NT, GW)
    BA, DT, G, BETA = (cr.take(NT, 4 * NH), cr.take(NT, 2 * NH), cr.take(NT, 2 * NH), cr.take(NT, 2 * NH))
    top = cr.at
    U, C = cr.take(6, TOK), cr.take(6, TOK)
    project(nc, k, ctx, Carve(cr.arena, cr.at), w_in, "dn", [
        (D_QKV, 384, U[:, 0:3], False), (D_QKV + 384, 384, U[:, 3:6], False), (D_Z, GW, Z, True),
        (D_BA, 4 * NH, BA, True)])
    conv_silu(nc, k, ctx, Carve(cr.arena, cr.at), "dn", U, C, T, conv_w, None, (0, 1, 2, 3, 4, 5))
    decay_rates(nc, k, ctx, Carve(cr.arena, top), "dn", BA[:, :, 2 * NH:], dt_bias, a_log, DT, G,
                BA[:, :, 0:2 * NH], BETA)

    cr = Carve(cr.arena, top)
    SQ = cr.take(NT, 2 * GW)
    ss, rs, rt = (cr.take(NT * 2 * NH) for _ in range(3))
    nch = sem("norm_chain")
    with nc.Block() as block:
        @block.vector
        def _(dve):
            chain = Chain(dve, nch)
            chain(nc.vector.tensor_tensor(SQ, T[:, :, 0:2 * GW], T[:, :, 0:2 * GW], ALU.mult))
            chain(nc.vector.tensor_reduce(ss, SQ.rearrange("p t (h d) -> p (t h) d", d=HD), AX.X, ALU.add))
            chain(nc.vector.tensor_scalar(ss, ss, 1e-6, None, ALU.add))
            rsqrt(nc, chain, ss, rs, rt)
            r3 = rs.rearrange("p (t h) -> p t h", t=NT)
            chain(nc.vector.tensor_scalar(r3[:, :, 0:NH], r3[:, :, 0:NH], HD ** -0.5, None, ALU.mult))
            for h in range(2 * NH):
                c = slice(h * HD, (h + 1) * HD)
                last = nc.vector.tensor_tensor(T[:, :, c], T[:, :, c], over(r3[:, :, h], HD), ALU.mult)
            chain(last)

    cr = Carve(cr.arena, top)
    O = cr.take(2, NT, GW)
    top = cr.at
    bank = lambda d, n: k.ps[4 * d + n]
    inv = Inverse(nc, k, sem, cr, bank)
    GC, SM, EX, GL = cr.take(2, NH), cr.take(2, 3 * NH), cr.take(2, 3 * NH), cr.take(2, 2)
    LT, L, AQ = (cr.take(2, NH, P) for _ in range(3))
    TM = cr.take(2, 6 * P)
    KT = cr.take(2, 2, P)
    KBT, QT = cr.take(2, NH, P), cr.take(2, NH, P)
    BV, KD, RHS, UU, QS, t1 = (cr.take(2, GW) for _ in range(6))
    S, t2 = cr.take(2, 2, HD), cr.take(2, 2, HD)
    pe_s, act_s, dve_s, vch, zeroed = (sem("pe_stage"), sem("act_stage"), sem("dve_stage"), sem("dve_chain"),
                                       sem("zeroed"))
    SUMS, TURN, GRAM, SOLVE, OUT, NPE = 0, 1, 2, 3, 4, 5
    TURNED, EXPS, NACT = 0, 1, 2
    LOAD, CAPS, GRAMS, UOUT, CLOSE, NDVE = 0, 1, 2, 3, 4, 5
    at = lambda i, stage, d, n: i * (2 * n) + (2 * stage + d + 1)
    tile = lambda i, d: i if d == 0 else (NT + 1 - i) % NT
    hv = heads
    with nc.Block() as block:
        @block.tensor
        def _(pe):
            with pe.Fori(0, NT) as i:
                for d in range(2):
                    hold(pe, dve_s, at(i, LOAD, d, NDVE))
                    for h in range(NH):
                        nc.tensor.matmul(bank(d, 0)[:, h * P:(h + 1) * P], GC[:, d, h:h + 1].to_broadcast([P, P]),
                                         k.incl[d], start=True, stop=True)
                    nc.tensor.matmul(bank(d, 1)[:, 0:NH], k.incl[d], GC[:, d], start=True, stop=True)
                    nc.tensor.matmul(bank(d, 1)[:, NH:2 * NH], k.ones, GC[:, d], start=True,
                                     stop=True).then_inc(pe_s, 1)
                for d in range(2):
                    for n in range(6):
                        last = nc.tensor.transpose(bank(d, 2 + n // 4)[:, (n % 4) * P:(n % 4 + 1) * P],
                                                   TM[:, d, n * P:(n + 1) * P], k.ident)
                    last.then_inc(pe_s, 1)
                for d in range(2):
                    hold(pe, act_s, at(i, TURNED, d, NACT))
                    hold(pe, dve_s, at(i, CAPS, d, NDVE))
                    for h in range(NH):
                        c = slice(h * P, (h + 1) * P)
                        kt = KT[:, d, h // 2]
                        nc.tensor.matmul(bank(d, 0)[:, c], kt, KBT[:, d, h], start=True, stop=True)
                        nc.tensor.matmul(bank(d, 1)[:, c], KBT[:, d, h], kt, start=True, stop=True)
                        nc.tensor.matmul(bank(d, 2)[:, c], kt, QT[:, d, h], start=True, stop=True)
                        s = S[:, d, h // 2]
                        nc.tensor.matmul(bank(d, 3)[:, h * HD:(h + 1) * HD], KBT[:, d, h], s, start=True, stop=True)
                        last = nc.tensor.matmul(bank(d, 3)[:, GW + h * HD:GW + (h + 1) * HD], QT[:, d, h], s,
                                                start=True, stop=True)
                    last.then_inc(pe_s, 1)
                inv.tensor(pe, i, dve_s, lambda d: at(i, GRAMS, d, NDVE))
                for d in range(2):
                    inv.solved(pe, i, d)
                    for h in range(NH):
                        c = slice(h * HD, (h + 1) * HD)
                        last = nc.tensor.matmul(bank(d, 3)[:, c], inv.Y[:, d, h], RHS[:, d, c], start=True, stop=True)
                    last.then_inc(pe_s, 1)
                for d in range(2):
                    hold(pe, dve_s, at(i, UOUT, d, NDVE))
                    for h in range(NH):
                        c = slice(h * HD, (h + 1) * HD)
                        r = slice(HD * (h % 2), HD * (h % 2) + HD)
                        nc.tensor.matmul(bank(d, 0)[:, c], AQ[:, d, h], UU[:, d, c], start=True, stop=True)
                        last = nc.tensor.matmul(bank(d, 1)[r, (h // 2) * HD:(h // 2 + 1) * HD], KD[:, d, c],
                                                UU[:, d, c], start=True, stop=True)
                    last.then_inc(pe_s, 1)

        @block.gpsimd
        def _(pool):
            with pool.Fori(0, NT) as i:
                inv.pool(pool, i, dve_s, lambda d: at(i, GRAMS, d, NDVE))

        @block.scalar
        def _(act):
            act.wait_ge(zeroed, 2)
            with act.Fori(0, NT) as i:
                for d in range(2):
                    hold(act, pe_s, at(i, TURN, d, NPE))
                    b2, b3 = heads(bank(d, 2)), heads(bank(d, 3))
                    nc.scalar.copy(KT[:, d], b2[:, 0:2])
                    nc.scalar.copy(KBT[0:HD, d, 0::2], b2[0:HD, 2:4])
                    nc.scalar.copy(KBT[HD:P, d, 1::2], b2[HD:P, 2:4])
                    nc.scalar.copy(QT[0:HD, d, 0::2], b3[0:HD, 0:2])
                    nc.scalar.copy(QT[HD:P, d, 1::2], b3[HD:P, 0:2]).then_inc(act_s, 1)
                for d in range(2):
                    hold(act, dve_s, at(i, CAPS, d, NDVE))
                    nc.scalar.activation(LT[:, d], LT[:, d], ACT.Exp)
                    nc.scalar.activation(L[:, d], L[:, d], ACT.Exp, scale=-1.0)
                    nc.scalar.activation(EX[:, d], SM[:, d], ACT.Exp).then_inc(act_s, 1)
                inv.scalar(act, i)

        @block.vector
        def _(dve):
            chain = Chain(dve, vch)
            chain(nc.vector.memset(S, 0.0))
            nc.vector.memset(KBT, 0.0).then_inc(zeroed, 1)
            nc.vector.memset(QT, 0.0).then_inc(zeroed, 1)
            with dve.Fori(0, NT) as i:
                chain.enter(i, 10)
                for d in range(2):
                    t = tile(i, d)
                    beta = over(BETA[:, t, d * NH:(d + 1) * NH], HD)
                    nc.vector.tensor_copy(GC[:, d], G[:, t, d * NH:(d + 1) * NH])
                    nc.vector.tensor_copy(TM[:, d, 0:GW], T[:, t, GW:2 * GW])
                    nc.vector.tensor_tensor(hv(TM[:, d, GW:2 * GW]), hv(T[:, t, GW:2 * GW]), beta, ALU.mult)
                    nc.vector.tensor_tensor(hv(BV[:, d]), hv(T[:, t, 2 * GW:]), beta, ALU.mult)
                    nc.vector.tensor_copy(TM[:, d, 2 * GW:], T[:, t, 0:GW]).then_inc(dve_s, 1)
                for d in range(2):
                    hold(dve, pe_s, at(i, SUMS, d, NPE))
                    nc.vector.tensor_copy(SM[:, d, 0:NH], bank(d, 1)[:, 0:NH])
                    chain(nc.vector.tensor_copy(SM[:, d, 2 * NH:], bank(d, 1)[:, NH:2 * NH]))
                    nc.vector.tensor_tensor(SM[:, d, NH:2 * NH], SM[:, d, 2 * NH:], SM[:, d, 0:NH], ALU.subtract)
                    for h in range(NH):
                        g = bank(d, 0)[:, h * P:(h + 1) * P]
                        nc.vector.scalar_tensor_tensor(LT[:, d, h], g, SM[:, d, h:h + 1], k.cap[d],
                                                       ALU.subtract, ALU.min)
                        last = nc.vector.scalar_tensor_tensor(L[:, d, h], g, SM[:, d, h:h + 1], k.floor[d],
                                                              ALU.subtract, ALU.max)
                    last.then_inc(dve_s, 1)
                for d in range(2):
                    hold(dve, act_s, at(i, EXPS, d, NACT))
                    hold(dve, pe_s, at(i, GRAM, d, NPE))
                    b = lambda n: heads(bank(d, n))
                    STT = nc.vector.scalar_tensor_tensor
                    STT(inv.DT[:, d], b(0), -1.0, LT[:, d], ALU.mult, ALU.mult)
                    chain(STT(inv.N[:, d], b(1), -1.0, L[:, d], ALU.mult, ALU.mult))
                    nc.vector.tensor_tensor(inv.D[:, d], inv.N[:, d], each(k.blk[16], NH), ALU.mult)
                    chain(nc.vector.tensor_tensor(inv.DT[:, d], inv.DT[:, d], each(k.dmaskT[d], NH), ALU.mult))
                    nc.vector.tensor_tensor(inv.Y[:, d], inv.DT[:, d], each(k.ident, NH), ALU.add)
                    nc.vector.tensor_tensor(AQ[:, d], b(2), LT[:, d], ALU.mult)
                    chain(nc.vector.tensor_tensor(hv(t1[:, d]), hv(bank(d, 3)[:, 0:GW]), over(EX[:, d, 0:NH], HD),
                                                  ALU.mult))
                    nc.vector.tensor_tensor(RHS[:, d], BV[:, d], t1[:, d], ALU.subtract)
                    nc.vector.tensor_tensor(hv(QS[:, d]), hv(bank(d, 3)[:, GW:2 * GW]), over(EX[:, d, 0:NH], HD),
                                            ALU.mult)
                    nc.vector.tensor_tensor(hv(KD[:, d]), hv(TM[:, d, 0:GW]), over(EX[:, d, NH:2 * NH], HD), ALU.mult)
                    nc.vector.tensor_copy(GL[0:HD, d], EX[0:HD, d, 2 * NH::2])
                    chain(nc.vector.tensor_copy(GL[HD:P, d], EX[HD:P, d, 2 * NH + 1::2]))
                    nc.vector.tensor_tensor(t2[:, d], S[:, d], over(GL[:, d], HD), ALU.mult).then_inc(dve_s, 1)
                inv.vector(dve, i)
                for d in range(2):
                    hold(dve, pe_s, at(i, SOLVE, d, NPE))
                    nc.vector.tensor_copy(UU[:, d], bank(d, 3)[:, 0:GW]).then_inc(dve_s, 1)
                for d in range(2):
                    hold(dve, pe_s, at(i, OUT, d, NPE))
                    nc.vector.tensor_tensor(O[:, d, tile(i, d), :], QS[:, d], bank(d, 0)[:, 0:GW], ALU.add)
                    nc.vector.tensor_tensor(S[:, d], t2[:, d], bank(d, 1)[:, 0:P].rearrange("p (q v) -> p q v", q=2),
                                            ALU.add).then_inc(dve_s, 1)
                    hold(dve, dve_s, at(i, CLOSE, d, NDVE))
                chain.leave(NT)

    head_norm_gate(nc, k, ctx, Carve(cr.arena, top), "dn", O, Z[:, CT:, :], norm_g, y_dram, 3)


def rwkv(nc, k, ctx, cr, low, w_in, w_w2, w0, a_w2, a0, g_w2, k_k, k_a, r_k, ln_g, ln_b, y_dram):
    sem = lambda n: ctx.semaphore("rwkv_" + n)
    RKV = cr.take(NT, 3 * GW)
    LW = cr.take(NT, 2 * GW)
    KK, B = cr.take(NT, GW), cr.take(NT, GW)
    GATE = cr.take(XT, GW)
    DEC = cr.take(2, NT, 2)
    top = cr.at
    A = cr.take(NT, GW)
    wT, aT, gT = (cr.take(TOK) for _ in range(3))
    project(nc, k, ctx, Carve(cr.arena, cr.at), w_in, "rwkv", [
        (B_R, 512, RKV[:, :, 0:512], True), (B_R + 512, 256, RKV[:, :, 512:768], True),
        (B_WL, 64, wT, False), (B_WL + 64, 32, aT, False), (B_GL, 64, gT, False)])

    W2, A2, G2 = cr.take(2 * GW), cr.take(GW), cr.take(GW)
    vec = cr.take(3, GW)
    SQ = cr.take(NT, GW)
    ss, rs, rt = (cr.take(NT * NH) for _ in range(3))
    w_zero, w_in_s, v_in, act_in, mm, sig, lwr, dsum, vch = (
        sem("w2_zeroed"), sem("w2_loaded"), sem("vectors_loaded"), sem("lowrank_ready"), sem("logits_ready"),
        sem("sigmoids_out"), sem("log_decays_ready"), sem("decay_sums"), sem("prep_chain"))
    ach = sem("act_chain")
    with nc.Block() as block:
        @block.sync
        def _(sp):
            sp.wait_ge(w_zero, 3)
            for d in range(2):
                sp.dma_start(W2[32 * d:32 * d + 32, d * GW:(d + 1) * GW], w_w2[0, d]).then_inc(w_in_s, 16)
            sp.dma_start(W2[64:65, :], w0.rearrange("a d n -> a (d n)")).then_inc(w_in_s, 16)
            sp.dma_start(A2[0:32, :], a_w2[0]).then_inc(w_in_s, 16)
            sp.dma_start(A2[32:33, :], a0).then_inc(w_in_s, 16)
            sp.dma_start(G2[0:64, :], g_w2[0]).then_inc(w_in_s, 16)
            sp.dma_start(vec[:, 0], k_k[0:1, :].to_broadcast([P, GW])).then_inc(v_in, 16)
            sp.dma_start(vec[:, 1], k_a[0:1, :].to_broadcast([P, GW])).then_inc(v_in, 16)

        @block.scalar
        def _(act):
            chain = Chain(act, ach)
            chain(nc.scalar.activation(wT[0:64, :], wT[0:64, :], ACT.Tanh))
            nc.scalar.activation(gT[0:64, :], gT[0:64, :], ACT.Sigmoid).then_inc(act_in, 1)
            for t in range(NT):
                act.wait_ge(mm, t + 1)
                b = [k.ps[2 * (t % 4) + n] for n in range(2)]
                nc.scalar.activation(LW[:, t, :], b[0], ACT.Sigmoid)
                if t >= CT:
                    nc.scalar.copy(GATE[:, t - CT, :], b[1][:, GW:2 * GW])
                nc.scalar.activation(A[:, t, :], b[1][:, 0:GW], ACT.Sigmoid).then_inc(sig, 1)
            act.wait_ge(dsum, 1)
            chain(nc.scalar.activation(DEC, k.ps[0][:, 0:4 * NT].rearrange("p (d t q) -> p d t q", d=2, t=NT),
                                       ACT.Exp))

        @block.tensor
        def _(pe):
            pe.wait_ge(w_in_s, 96)
            pe.wait_ge(act_in, 1)
            for t in range(NT):
                if t >= 4:
                    pe.wait_ge(sig, t - 3)
                c = slice(t * P, (t + 1) * P)
                b = [k.ps[2 * (t % 4) + n] for n in range(2)]
                nc.tensor.matmul(b[0][:, :], wT[0:65, c], W2[0:65, :], start=True, stop=True)
                nc.tensor.matmul(b[1][:, GW:2 * GW], gT[0:64, c], G2[0:64, :], start=True, stop=True)
                nc.tensor.matmul(b[1][:, 0:GW], aT[0:33, c], A2[0:33, :], start=True, stop=True).then_inc(mm, 1)
            pe.wait_ge(lwr, 1)
            pe.wait_ge(sig, NT)
            for d in range(2):
                for t in range(NT):
                    for p in range(2):
                        at = (d * NT + t) * 2 + p
                        last = nc.tensor.matmul(k.ps[0][:, at:at + 1], LW[:, t, d * GW + p * P:d * GW + (p + 1) * P],
                                                k.ones[:, 0:1], start=True, stop=True)
            last.then_inc(dsum, 1)

        @block.vector
        def _(dve):
            chain = Chain(dve, vch)
            nc.vector.memset(W2[0:64, :], 0.0).then_inc(w_zero, 1)
            nc.vector.memset(wT[64:65, :], 1.0).then_inc(w_zero, 1)
            nc.vector.memset(aT[32:33, :], 1.0).then_inc(w_zero, 1)
            dve.wait_ge(v_in, 32)
            K = RKV[:, :, GW:2 * GW]
            hv3 = lambda b: b.rearrange("p t (h d) -> p (t h) d", d=HD)
            chain(nc.vector.tensor_tensor(KK, K, each(vec[:, 0], NT), ALU.mult))
            chain(nc.vector.tensor_tensor(SQ, KK, KK, ALU.mult))
            chain(nc.vector.tensor_reduce(ss, hv3(SQ), AX.X, ALU.add))
            chain(nc.vector.tensor_scalar(ss, ss, 1e-6, None, ALU.add))
            rsqrt(nc, chain, ss, rs, rt)
            chain(nc.vector.tensor_tensor(hv3(KK), hv3(KK), over(rs, HD), ALU.mult))
            dve.wait_ge(sig, NT)
            nc.vector.tensor_scalar(LW, LW, -(2.718281828459045 ** -0.5), None, ALU.mult).then_inc(lwr, 1)
            chain(nc.vector.tensor_tensor(B, KK, A, ALU.mult))
            chain(nc.vector.tensor_scalar(A, A, 1.0, None, ALU.subtract))
            chain(nc.vector.tensor_tensor(A, A, each(vec[:, 1], NT), ALU.mult))
            chain(nc.vector.tensor_scalar(A, A, 1.0, None, ALU.add))
            chain(nc.vector.tensor_tensor(K, K, A, ALU.mult))

    cr = Carve(cr.arena, top)
    O = cr.take(2, NT, GW)
    after = cr.at
    lo = Carve(cr.arena, low)
    bank = lambda d, n: k.ps[4 * d + n]
    inv = Inverse(nc, k, sem, lo, bank)
    EG = inv.X.rearrange("p e h n -> p e (h n)")
    EX = inv.T1.rearrange("p e h n -> p e (h n)")
    AZK, ABR, AKR, ZT, RT = (cr.take(2, NH, P) for _ in range(5))
    KT, BT = cr.take(2, 2, P), cr.take(2, 2, P)
    TM = cr.take(2, 4 * GW)
    V, RHS, UU = (cr.take(2, GW) for _ in range(3))
    S, t2 = cr.take(2, 2, HD), cr.take(2, 2, HD)
    pe_s, act_s, dve_s, lch, zeroed = (sem("pe_stage"), sem("act_stage"), sem("dve_stage"), sem("dve_chain"),
                                       sem("zeroed"))
    SUMS, TURN, GRAM, GRAMB, RIGHT, SOLVE, OUT, NPE = 0, 1, 2, 3, 4, 5, 6, 7
    EXPS, TURNED, NACT = 0, 1, 2
    BEFORE, SCALED, GRAMS, GRAMBS, RIGHTS, UOUT, CLOSE, NDVE = 0, 1, 2, 3, 4, 5, 6, 7
    at = lambda i, stage, d, n: i * (2 * n) + (2 * stage + d + 1)
    tile = lambda i, d: i if d == 0 else (NT + 1 - i) % NT
    with nc.Block() as block:
        @block.tensor
        def _(pe):
            with pe.Fori(0, NT) as i:
                for d in range(2):
                    nc.tensor.matmul(bank(d, 3)[:, 0:GW], k.incl[d], LW[:, tile(i, d), d * GW:(d + 1) * GW],
                                     start=True, stop=True).then_inc(pe_s, 1)
                for d in range(2):
                    hold(pe, dve_s, at(i, SCALED, d, NDVE))
                    for n in range(8):
                        last = nc.tensor.transpose(bank(d, 1 + n // 4)[:, (n % 4) * P:(n % 4 + 1) * P],
                                                   TM[:, d, n * P:(n + 1) * P], k.ident)
                    last.then_inc(pe_s, 1)
                for d in range(2):
                    hold(pe, act_s, at(i, TURNED, d, NACT))
                    for h in range(NH):
                        c = slice(h * P, (h + 1) * P)
                        q = h // 2
                        nc.tensor.matmul(bank(d, 0)[:, c], BT[:, d, q], ZT[:, d, h], start=True, stop=True)
                        nc.tensor.matmul(bank(d, 1)[:, c], ZT[:, d, h], BT[:, d, q], start=True, stop=True)
                        nc.tensor.matmul(bank(d, 2)[:, c], KT[:, d, q], ZT[:, d, h], start=True, stop=True)
                        last = nc.tensor.matmul(bank(d, 3)[:, c], BT[:, d, q], RT[:, d, h], start=True, stop=True)
                    last.then_inc(pe_s, 1)
                for d in range(2):
                    hold(pe, dve_s, at(i, GRAMS, d, NDVE))
                    for h in range(NH):
                        last = nc.tensor.matmul(bank(d, 3)[:, h * P:(h + 1) * P], KT[:, d, h // 2], RT[:, d, h],
                                                start=True, stop=True)
                    last.then_inc(pe_s, 1)
                for d in range(2):
                    hold(pe, dve_s, at(i, GRAMBS, d, NDVE))
                    for h in range(NH):
                        c = slice(h * HD, (h + 1) * HD)
                        nc.tensor.matmul(bank(d, 3)[:, c], AZK[:, d, h], V[:, d, c], start=True, stop=False)
                        last = nc.tensor.matmul(bank(d, 3)[:, c], ZT[:, d, h], S[:, d, h // 2], start=False, stop=True)
                    last.then_inc(pe_s, 1)
                inv.tensor(pe, i, dve_s, lambda d: at(i, GRAMS, d, NDVE))
                for d in range(2):
                    inv.solved(pe, i, d)
                    hold(pe, dve_s, at(i, RIGHTS, d, NDVE))
                    for h in range(NH):
                        c = slice(h * HD, (h + 1) * HD)
                        last = nc.tensor.matmul(bank(d, 3)[:, c], inv.Y[:, d, h], RHS[:, d, c], start=True, stop=True)
                    last.then_inc(pe_s, 1)
                for d in range(2):
                    hold(pe, dve_s, at(i, UOUT, d, NDVE))
                    for h in range(NH):
                        c = slice(h * HD, (h + 1) * HD)
                        r = slice(HD * (h % 2), HD * (h % 2) + HD)
                        o = bank(d, 0)[:, c]
                        nc.tensor.matmul(o, ABR[:, d, h], UU[:, d, c], start=True, stop=False)
                        nc.tensor.matmul(o, AKR[:, d, h], V[:, d, c], start=False, stop=False)
                        nc.tensor.matmul(o, RT[:, d, h], S[:, d, h // 2], start=False, stop=True)
                        s = bank(d, 1)[r, (h // 2) * HD:(h // 2 + 1) * HD]
                        b = lambda n: TM[:, d, n * GW + h * HD:n * GW + (h + 1) * HD]
                        nc.tensor.matmul(s, b(1), UU[:, d, c], start=True, stop=False)
                        last = nc.tensor.matmul(s, b(3), V[:, d, c], start=False, stop=True)
                    last.then_inc(pe_s, 1)

        @block.gpsimd
        def _(pool):
            with pool.Fori(0, NT) as i:
                inv.pool(pool, i, dve_s, lambda d: at(i, GRAMS, d, NDVE))

        @block.scalar
        def _(act):
            act.wait_ge(zeroed, 2)
            with act.Fori(0, NT) as i:
                for d in range(2):
                    hold(act, dve_s, at(i, BEFORE, d, NDVE))
                    nc.scalar.activation(EG[:, d, 0:GW], bank(d, 3)[:, 0:GW], ACT.Exp)
                    nc.scalar.activation(EG[:, d, GW:], bank(d, 3)[:, 0:GW], ACT.Exp, scale=-1.0)
                    nc.scalar.activation(EX[:, d, GW:], EX[:, d, 0:GW], ACT.Exp).then_inc(act_s, 1)
                for d in range(2):
                    hold(act, pe_s, at(i, TURN, d, NPE))
                    for b, padded, pair in ((heads(bank(d, 1)), ZT, BT), (heads(bank(d, 2)), RT, KT)):
                        nc.scalar.copy(padded[0:HD, d, 0::2], b[0:HD, 0:2])
                        nc.scalar.copy(padded[HD:P, d, 1::2], b[HD:P, 0:2])
                        last = nc.scalar.copy(pair[:, d], b[:, 2:4])
                    last.then_inc(act_s, 1)
                inv.scalar(act, i)

        @block.vector
        def _(dve):
            chain = Chain(dve, lch)
            chain(nc.vector.memset(S, 0.0))
            nc.vector.memset(ZT, 0.0).then_inc(zeroed, 1)
            nc.vector.memset(RT, 0.0).then_inc(zeroed, 1)
            with dve.Fori(0, NT) as i:
                chain.enter(i, 4)
                TT, STT = nc.vector.tensor_tensor, nc.vector.scalar_tensor_tensor
                for d in range(2):
                    hold(dve, pe_s, at(i, SUMS, d, NPE))
                    TT(EX[:, d, 0:GW], bank(d, 3)[:, 0:GW], LW[:, tile(i, d), d * GW:(d + 1) * GW],
                       ALU.subtract).then_inc(dve_s, 1)
                for d in range(2):
                    t = tile(i, d)
                    hold(dve, act_s, at(i, EXPS, d, NACT))
                    to = lambda n: TM[:, d, n * GW:(n + 1) * GW]
                    STT(to(0), KK[:, t, :], -1.0, EX[:, d, GW:], ALU.mult, ALU.mult)
                    TT(to(1), B[:, t, :], EG[:, d, GW:], ALU.mult)
                    TT(to(2), RKV[:, t, 0:GW], EG[:, d, 0:GW], ALU.mult)
                    TT(to(3), RKV[:, t, GW:2 * GW], EG[:, d, GW:], ALU.mult)
                    nc.vector.tensor_copy(V[:, d], RKV[:, t, 2 * GW:]).then_inc(dve_s, 1)
                for d in range(2):
                    hold(dve, pe_s, at(i, GRAM, d, NPE))
                    b = lambda n: heads(bank(d, n))
                    TT(inv.DT[:, d], b(0), each(k.dmaskT[d], NH), ALU.mult)
                    chain(TT(inv.N[:, d], b(1), each(k.strict[d], NH), ALU.mult))
                    TT(inv.Y[:, d], inv.DT[:, d], each(k.ident, NH), ALU.add)
                    TT(inv.D[:, d], inv.N[:, d], each(k.blk[16], NH), ALU.mult)
                    TT(AZK[:, d], b(2), each(k.strictT[d], NH), ALU.mult)
                    TT(ABR[:, d], b(3), each(k.incl[d], NH), ALU.mult).then_inc(dve_s, 1)
                for d in range(2):
                    hold(dve, pe_s, at(i, GRAMB, d, NPE))
                    TT(AKR[:, d], heads(bank(d, 3)), each(k.incl[d], NH), ALU.mult).then_inc(dve_s, 1)
                for d in range(2):
                    hold(dve, pe_s, at(i, RIGHT, d, NPE))
                    nc.vector.tensor_copy(RHS[:, d], bank(d, 3)[:, 0:GW]).then_inc(dve_s, 1)
                inv.vector(dve, i)
                for d in range(2):
                    hold(dve, pe_s, at(i, SOLVE, d, NPE))
                    nc.vector.tensor_copy(UU[:, d], bank(d, 3)[:, 0:GW]).then_inc(dve_s, 1)
                for d in range(2):
                    hold(dve, pe_s, at(i, OUT, d, NPE))
                    nc.vector.tensor_copy(O[:, d, tile(i, d), :], bank(d, 0)[:, 0:GW])
                    chain(TT(t2[:, d], S[:, d], bank(d, 1)[:, 0:P].rearrange("p (q v) -> p q v", q=2), ALU.add))
                    TT(S[:, d], t2[:, d], over(DEC[:, d, tile(i, d), :], HD), ALU.mult).then_inc(dve_s, 1)
                    hold(dve, dve_s, at(i, CLOSE, d, NDVE))
                chain.leave(NT)

    cr = Carve(cr.arena, after)
    par_in, ready, written, pch = sem("post_loaded"), sem("post_ready"), sem("post_written"), sem("post_chain")
    lg, lb, rk = (cr.take(GW) for _ in range(3))
    Y, SQ, BO = (cr.take(XT, GW) for _ in range(3))
    ss, rs, rt = (cr.take(XT * NH) for _ in range(3))
    hv3 = lambda b: b.rearrange("p t (h d) -> p (t h) d", d=HD)
    with nc.Block() as block:
        @block.sync
        def _(sp):
            sp.dma_start(lg, ln_g[0:1, :].to_broadcast([P, GW])).then_inc(par_in, 16)
            sp.dma_start(lb, ln_b[0:1, :].to_broadcast([P, GW])).then_inc(par_in, 16)
            sp.dma_start(rk, r_k.rearrange("a h d -> a (h d)").to_broadcast([P, GW])).then_inc(par_in, 16)
            sp.wait_ge(ready, 1)
            write_out(sp, Y, y_dram, 1, written)

        @block.vector
        def _(dve):
            chain = Chain(dve, pch)
            TT = nc.vector.tensor_tensor
            R = lambda n: RKV[:, CT:, n * GW:(n + 1) * GW]
            chain(TT(Y, O[:, 0, CT:, :], O[:, 1, CT:, :], ALU.add))
            chain(nc.vector.tensor_reduce(ss, hv3(Y), AX.X, ALU.add))
            chain(nc.vector.tensor_scalar(ss, ss, 1.0 / HD, None, ALU.mult))
            chain(TT(hv3(Y), hv3(Y), over(ss, HD), ALU.subtract))
            chain(TT(SQ, Y, Y, ALU.mult))
            chain(nc.vector.tensor_reduce(ss, hv3(SQ), AX.X, ALU.add))
            chain(nc.vector.tensor_scalar(ss, ss, 1.0 / HD, GN_EPS, ALU.mult, ALU.add))
            rsqrt(nc, chain, ss, rs, rt)
            chain(TT(hv3(Y), hv3(Y), over(rs, HD), ALU.mult))
            dve.wait_ge(par_in, 48)
            chain(TT(Y, Y, each(lg, XT), ALU.mult))
            chain(TT(Y, Y, each(lb, XT), ALU.add))
            chain(TT(BO, R(0), R(1), ALU.mult))
            chain(TT(BO, BO, each(rk, XT), ALU.mult))
            chain(nc.vector.tensor_reduce(ss, hv3(BO), AX.X, ALU.add))
            for h in range(NH):
                c = slice(h * HD, (h + 1) * HD)
                last = TT(BO[:, :, c], R(2)[:, :, c], over(ss.rearrange("p (t h) -> p t h", h=NH)[:, :, h], HD),
                          ALU.mult)
            chain(last)
            chain(TT(Y, Y, BO, ALU.add))
            TT(Y, Y, GATE, ALU.mult).then_inc(ready, 1)


def mixed_out(nc, k, ctx, cr, x, w_out, y_dram, xn_dram, X1, HT):
    sem = lambda n: ctx.semaphore("mix_" + n)
    w_in, y_in, x_in = sem("w_loaded"), [sem("y_even"), sem("y_odd")], [sem("x_even"), sem("x_odd")]
    yt, mm, xt = sem("y_turned"), sem("product_done"), sem("xn_turned")
    ya, yd, x1, sq, xn, ha, hd, st, vch = (sem("yT_by_act"), sem("yT_by_dve"), sem("x1_ready"), sem("squares"),
                                           sem("xn_ready"), sem("h_by_act"), sem("h_by_dve"), [sem("xn_even_stored"), sem("xn_odd_stored")],
                                           sem("chain"))
    W = cr.take(KC, D)
    Y, X, YT, XN, junk = (cr.take(2, D) for _ in range(5))
    ss, rs, ri = (cr.take(2, 1) for _ in range(3))
    rt = cr.take(1)
    ps = k.ps
    with nc.Block() as block:
        @block.sync
        def _(sp):
            for t in range(XT):
                if t >= 2:
                    sp.wait_ge(yt, t - 1)
                sp.dma_start(Y[:, t % 2], y_dram[t * P:(t + 1) * P, :]).then_inc(y_in[t % 2], 16)
                if t == 0:
                    sp.dma_start(W, w_out[0].rearrange("(p c) n -> p c n", c=KC)).then_inc(w_in, 16)
                if t >= 2:
                    sp.wait_ge(x1, t - 1)
                sp.dma_start(X[:, t % 2], x[0, t * P:(t + 1) * P, :]).then_inc(x_in[t % 2], 16)
                if t >= 1:
                    sp.wait_ge(xn, t)
                    sp.dma_start(xn_dram[(t - 1) * P:t * P, :], XN[:, (t - 1) % 2]).then_inc(st[(t - 1) % 2], 16)
            sp.wait_ge(xn, XT)
            sp.dma_start(xn_dram[(XT - 1) * P:XT * P, :], XN[:, (XT - 1) % 2]).then_inc(st[(XT - 1) % 2], 16)
            for s in st:
                sp.wait_ge(s, 16 * (XT // 2))

        @block.tensor
        def _(pe):
            pe.wait_ge(w_in, 16)
            for t in range(XT + 1):
                if t < XT:
                    pe.wait_ge(y_in[t % 2], 16 * (t // 2 + 1))
                    for c in range(KC):
                        last = nc.tensor.transpose(ps[c // 4][:, (c % 4) * P:(c % 4 + 1) * P], Y[:, t % 2, c::KC],
                                                   k.ident)
                    last.then_inc(yt, 1)
                    pe.wait_ge(ya, t + 1)
                    pe.wait_ge(yd, t + 1)
                    if t >= 1:
                        pe.wait_ge(x1, t)
                    for half in range(2):
                        for c in range(KC):
                            last = nc.tensor.matmul(ps[2 + half][:, :], YT[:, t % 2, c * P:(c + 1) * P],
                                                    W[:, c, half * 512:(half + 1) * 512],
                                                    start=(c == 0), stop=(c == KC - 1))
                    last.then_inc(mm, 1)
                if t >= 1:
                    u = t - 1
                    pe.wait_ge(xn, u + 1)
                    if u >= 1:
                        pe.wait_ge(ha, u)
                        pe.wait_ge(hd, u)
                    for c in range(KC):
                        last = nc.tensor.transpose(ps[4 + c // 4][:, (c % 4) * P:(c % 4 + 1) * P],
                                                   XN[:, u % 2, c::KC], k.ident)
                    last.then_inc(xt, 1)

        @block.scalar
        def _(act):
            for t in range(XT + 1):
                if t < XT:
                    act.wait_ge(yt, t + 1)
                    if t >= 2:
                        act.wait_ge(mm, t - 1)
                    nc.scalar.copy(YT[:, t % 2, 0:512], ps[0][:, :]).then_inc(ya, 1)
                if t >= 1:
                    u = t - 1
                    act.wait_ge(x1, u + 1)
                    if u >= 2:
                        act.wait_ge(xn, u - 1)
                    nc.scalar.activation(junk[:, u % 2], X1[:, u], ACT.Square, accum_out=ss[:, u % 2]).then_inc(sq, 1)
                    act.wait_ge(xt, u + 1)
                    for c in range(KC // 2):
                        last = nc.scalar.activation(HT[:, c, u * P:(u + 1) * P], ps[4][:, c * P:(c + 1) * P],
                                                    ACT.Identity, bias=k.add_col[1][0][:, c:c + 1],
                                                    scale=k.mul_col[1][0][:, c:c + 1])
                    last.then_inc(ha, 1)

        @block.vector
        def _(dve):
            chain = Chain(dve, vch)
            for t in range(XT + 1):
                if t < XT:
                    dve.wait_ge(yt, t + 1)
                    if t >= 2:
                        dve.wait_ge(mm, t - 1)
                    nc.vector.tensor_copy(YT[:, t % 2, 512:], ps[1][:, :]).then_inc(yd, 1)
                if t >= 1:
                    u = t - 1
                    dve.wait_ge(mm, u + 1)
                    for half in range(2):
                        c = slice(half * 512, (half + 1) * 512)
                        last = nc.vector.tensor_tensor(X1[:, u, c], ps[2 + half][:, :], k.gate[0][:, c], ALU.mult)
                    chain(last)
                    dve.wait_ge(x_in[u % 2], 16 * (u // 2 + 1))
                    nc.vector.tensor_tensor(X1[:, u], X1[:, u], X[:, u % 2], ALU.add).then_inc(x1, 1)
                    dve.wait_ge(sq, u + 1)
                    chain(nc.vector.tensor_scalar(rs[:, u % 2], ss[:, u % 2], 1.0 / D, RMS_EPS, ALU.mult, ALU.add))
                    rsqrt(nc, chain, rs[:, u % 2], ri[:, u % 2], rt)
                    if u >= 2:
                        dve.wait_ge(st[u % 2], 16 * (u // 2))
                        dve.wait_ge(xt, u - 1)
                    nc.vector.tensor_scalar(XN[:, u % 2], X1[:, u], ri[:, u % 2], None, ALU.mult).then_inc(xn, 1)
                    dve.wait_ge(xt, u + 1)
                    for c in range(KC // 2, KC):
                        last = nc.vector.tensor_scalar(HT[:, c, u * P:(u + 1) * P],
                                                       ps[5][:, (c - 4) * P:(c - 3) * P], k.mul_col[1][0][:, c:c + 1],
                                                       k.add_col[1][0][:, c:c + 1], ALU.mult, ALU.add)
                    last.then_inc(hd, 1)


def shared_and_scores(nc, k, ctx, cr, HT, router_w, router_b, wg, wu, wd, ACC, SC, SB):
    sem = lambda n: ctx.semaphore("shared_" + n)
    r_in, b_in, gu_in, d_in = sem("router_loaded"), sem("bias_loaded"), sem("gate_up_loaded"), sem("down_loaded")
    lg, sc, up, sil, hid, dn, vch = (sem("logits_ready"), sem("scores_ready"), sem("up_done"), sem("silu_done"),
                                     sem("hidden_ready"), sem("down_done"), sem("chain"))
    out = [sem("out_by_act"), sem("out_by_dve")]
    RW, RB = cr.take(KC, NE), cr.take(NE)
    WG, WU, WD = cr.take(KC, ED), cr.take(KC, ED), cr.take(2, D)
    HID = cr.take(2, SEQ)
    SG = cr.take(2, 512)
    kc = lambda w: w.rearrange("(p c) n -> p c n", c=KC)
    with nc.Block() as block:
        @block.sync
        def _(sp):
            sp.dma_start(RW, kc(router_w[0])).then_inc(r_in, 16)
            sp.dma_start(RB, router_b[0:1, :].to_broadcast([P, NE])).then_inc(b_in, 16)
            sp.dma_start(WG, kc(wg[0])).then_inc(gu_in, 16)
            sp.dma_start(WU, kc(wu[0])).then_inc(gu_in, 16)
            sp.dma_start(WD, wd[0].rearrange("(p c) n -> p c n", c=2)).then_inc(d_in, 16)

        @block.tensor
        def _(pe):
            pe.wait_ge(r_in, 16)
            for t in range(XT):
                for c in range(KC):
                    last = nc.tensor.matmul(k.ps[0][:, t * NE:(t + 1) * NE], HT[:, c, t * P:(t + 1) * P], RW[:, c],
                                            start=(c == 0), stop=(c == KC - 1))
            last.then_inc(lg, 1)
            pe.wait_ge(gu_in, 32)
            for n in range(4):
                f, a = n // 2, (n % 2) * 512
                if n >= 2:
                    pe.wait_ge(hid, n - 1)
                for b, W in ((1, WG), (2, WU)):
                    for c in range(KC):
                        last = nc.tensor.matmul(k.ps[b + 2 * (n % 2)][:, :], W[:, c, f::2], HT[:, c, a:a + 512],
                                                start=(c == 0), stop=(c == KC - 1))
                last.then_inc(up, 1)
            pe.wait_ge(d_in, 16)
            pe.wait_ge(hid, 4)
            for n in range(2 * XT):
                t, half = n // 2, n % 2
                if n >= 4:
                    pe.wait_ge(out[n % 2], (n - 4) // 2 + 1)
                for f in range(2):
                    last = nc.tensor.matmul(k.ps[1 + n % 4][:, :], HID[:, f, t * P:(t + 1) * P],
                                            WD[:, f, half * 512:(half + 1) * 512], start=(f == 0), stop=(f == 1))
                last.then_inc(dn, 1)

        @block.scalar
        def _(act):
            act.wait_ge(lg, 1)
            nc.scalar.activation(SC, k.ps[0][:, :].rearrange("p (t e) -> p t e", e=NE), ACT.Sigmoid).then_inc(sc, 1)
            for n in range(4):
                act.wait_ge(up, n + 1)
                if n >= 2:
                    act.wait_ge(hid, n - 1)
                nc.scalar.activation(SG[:, n % 2], k.ps[1 + 2 * (n % 2)][:, :], ACT.Silu).then_inc(sil, 1)
            for n in range(0, 2 * XT, 2):
                act.wait_ge(dn, n + 1)
                nc.scalar.copy(ACC[:, n // 2, 0:512], k.ps[1 + n % 4][:, :]).then_inc(out[0], 1)

        @block.vector
        def _(dve):
            chain = Chain(dve, vch)
            dve.wait_ge(sc, 1)
            dve.wait_ge(b_in, 16)
            chain(nc.vector.tensor_tensor(SB, SC, each(RB, XT), ALU.add))
            for n in range(4):
                f, a = n // 2, (n % 2) * 512
                dve.wait_ge(sil, n + 1)
                nc.vector.tensor_tensor(HID[:, f, a:a + 512], SG[:, n % 2], k.ps[2 + 2 * (n % 2)][:, :],
                                        ALU.mult).then_inc(hid, 1)
            for n in range(1, 2 * XT, 2):
                dve.wait_ge(dn, n + 1)
                nc.vector.tensor_copy(ACC[:, n // 2, 512:], k.ps[1 + n % 4][:, :]).then_inc(out[1], 1)


def dispatch(nc, k, ctx, cr, SC, SB, buf_dram, DST, WK, BEX, IDX):
    sem = lambda n: ctx.semaphore("disp_" + n)
    vch, m_ready, cum, zero, tok, dst, bex_t, bex_r, zeroed, scat, idx_in, idx_f, idx_t = (
        sem("chain"), sem("mask_ready"), sem("ranks_ready"), sem("zeros_made"), sem("token_ids_made"),
        sem("rows_ready"), sem("block_ends_counted"), sem("block_experts_turned"), sem("buffer_zeroed"),
        sem("ids_scattered"), sem("ids_loaded"), sem("ids_as_float"), sem("ids_turned"))
    M, W, RK, DS, R, SEL = (cr.take(XT, NE) for _ in range(6))
    RNK = cr.take(XT, NE)
    TOT = cr.take(XT, NE)
    T8 = cr.take(XT, 8)
    OFF, CNT, NB, END, ST, c1 = (cr.take(NE) for _ in range(6))
    ONE = cr.take(NE)
    den = cr.take(XT)
    DF = cr.take(XT, 8)
    blk = cr.take(1)
    nb_le = cr.take(NE)
    bx = cr.take(1)
    Z, TK = cr.take(P).bitcast(I32), cr.take(XT).bitcast(I32)
    IL, IF = cr.take(P).bitcast(I32), cr.take(P)
    BI = cr.take(1).bitcast(I32)
    flat = lambda b: b.rearrange("p t e -> p (t e)")
    with nc.Block() as block:
        @block.gpsimd
        def _(pool):
            nc.gpsimd.memset(Z, 0).then_inc(zero, 1)
            nc.gpsimd.iota(TK, [[P, XT]], base=0, channel_multiplier=1).then_inc(tok, 1)
            nc.gpsimd.iota(BI, [[0, 1]], base=0, channel_multiplier=1).then_inc(tok, 1)
            pool.wait_ge(tok, 2)
            pool.wait_ge(zeroed, 16)
            pool.wait_ge(dst, 1)
            for t in range(XT):
                for s in range(TOPK):
                    nc.gpsimd.indirect_dma_start(
                        out=buf_dram, out_offset=bass.IndirectOffsetOnAxis(ap=DST[:, t, s:s + 1], axis=0),
                        in_=TK[:, t:t + 1], in_offset=None).then_inc(scat, 16)
            pool.wait_ge(scat, 16 * XT * TOPK)

        @block.sync
        def _(sp):
            sp.wait_ge(zero, 1)
            sp.dma_start(buf_dram.rearrange("(a b) o -> a (b o)", a=P), Z).then_inc(zeroed, 16)
            sp.wait_ge(scat, 16 * XT * TOPK)
            sp.dma_start(IL, buf_dram.rearrange("(a b) o -> a (b o)", a=P)).then_inc(idx_in, 16)

        @block.tensor
        def _(pe):
            pe.wait_ge(m_ready, 1)
            nc.tensor.matmul(k.ps[0][:, :], k.gt, flat(M), start=True, stop=True)
            nc.tensor.matmul(k.ps[1][:, :], k.ones, flat(M), start=True, stop=True).then_inc(cum, 1)
            pe.wait_ge(bex_t, 1)
            nc.tensor.transpose(k.ps[2][0:1, 0:P], bx, k.ident).then_inc(bex_r, 1)
            pe.wait_ge(idx_f, 1)
            nc.tensor.transpose(k.ps[3][:, 0:P], IF, k.ident).then_inc(idx_t, 1)

        @block.vector
        def _(dve):
            chain = Chain(dve, vch)
            TT, TS, STT = nc.vector.tensor_tensor, nc.vector.tensor_scalar, nc.vector.scalar_tensor_tensor
            chain(nc.vector.memset(ONE, 1.0))
            for t in range(XT):
                last = nc.vector.max(T8[:, t], SB[:, t])
            chain(last)
            for t in range(XT):
                last = nc.vector.match_replace(RK[:, t], T8[:, t], SB[:, t], -BIG)
            chain(last)
            TT(M, RK, SB, ALU.not_equal).then_inc(m_ready, 1)
            dve.wait_ge(m_ready, 1)
            chain(TT(W, SC, M, ALU.mult))
            chain(nc.vector.tensor_reduce(den, W, AX.X, ALU.add))
            chain(nc.vector.reciprocal(den, den))
            chain(TS(den, den, 2.5, None, ALU.mult))
            chain(TT(W, W, over(den, NE), ALU.mult))
            for t in range(XT):
                last = nc.vector.tensor_tensor_scan(R[:, t], ONE, M[:, t], 0.0, ALU.mult, ALU.add)
            chain(last)
            chain(TT(R, R, M, ALU.mult))
            dve.wait_ge(cum, 1)
            nc.vector.tensor_copy(flat(RNK), k.ps[0][:, :])
            chain(nc.vector.tensor_copy(flat(TOT), k.ps[1][:, :]))
            chain(nc.vector.tensor_copy(OFF, TOT[:, 0]))
            for t in range(1, XT):
                chain(TT(RNK[:, t], RNK[:, t], OFF, ALU.add))
                chain(TT(OFF, OFF, TOT[:, t], ALU.add))
            chain(TS(NB, OFF, 0.0, None, ALU.is_gt))
            for b in range(1, SEQ // P):
                chain(STT(NB, OFF, float(b * P), NB, ALU.is_gt, ALU.add))
            chain(nc.vector.tensor_tensor_scan(END, ONE, NB, 0.0, ALU.mult, ALU.add))
            chain(TT(ST, END, NB, ALU.subtract))
            chain(TS(ST, ST, float(P), None, ALU.mult))
            chain(TT(DS, RNK, each(ST, XT), ALU.add))
            for s in range(TOPK):
                chain(STT(SEL, R, float(s + 1), DS, ALU.is_equal, ALU.mult))
                chain(nc.vector.tensor_reduce(DF[:, :, s], SEL, AX.X, ALU.add))
                chain(STT(SEL, R, float(s + 1), W, ALU.is_equal, ALU.mult))
                chain(nc.vector.tensor_reduce(WK[:, :, s], SEL, AX.X, ALU.add))
            nc.vector.tensor_copy(DST, DF).then_inc(dst, 1)
            dve.wait_ge(tok, 2)
            chain(nc.vector.tensor_copy(blk, BI))
            chain(TS(nb_le, END, blk, None, ALU.is_le))
            chain(nc.vector.tensor_reduce(bx, nb_le, AX.X, ALU.add))
            TS(bx, bx, float(NE - 1), None, ALU.min).then_inc(bex_t, 1)
            dve.wait_ge(bex_r, 1)
            chain(nc.vector.tensor_copy(BEX[0:1, :], k.ps[2][0:1, 0:P]))
            dve.wait_ge(idx_in, 16)
            nc.vector.tensor_copy(IF, IL).then_inc(idx_f, 1)
            dve.wait_ge(idx_t, 1)
            chain(nc.vector.tensor_copy(IDX[:, 0:NBLK], k.ps[3][:, 0:P]))


def experts(nc, k, ctx, cr, wg, wu, wd, xn_dram, y_dram, BEX, IDX):
    sem = lambda n: ctx.semaphore("exp_" + n)
    two = lambda n: [sem(n + "_even"), sem(n + "_odd")]
    gu_free, d_free, gu_in, d_in = two("gate_up_free"), two("down_free"), two("gate_up_loaded"), two("down_loaded")
    idx, g_in, turned, xa, xd = (two("index_ready"), two("rows_gathered"), two("rows_turned"), two("xT_by_act"),
                                 two("xT_by_dve"))
    up, sil, hid, ht, hto, dn, ya, yd, st = (two("up_done"), two("silu_done"), two("hidden_ready"),
                                             two("hidden_turned"), two("hiddenT_ready"), two("down_done"),
                                             two("y_by_act"), two("y_by_dve"), two("y_stored"))
    WGU, WD = cr.take(2, KC, 2 * ED), cr.take(2, 2, D)
    G, XTT, YB = cr.take(2, D), cr.take(2, KC, P), cr.take(2, D)
    SG, H, HT = cr.take(2, ED), cr.take(2, ED), cr.take(2, 2, P)
    ID = cr.take(2, 1).bitcast(I32)
    ps = k.ps
    PAIRS = NBLK // 2
    with nc.Block() as block:
        @block.sync
        def _(sp):
            for q in range(2):
                sp.sem_inc(gu_free[q], 1)
                sp.sem_inc(d_free[q], 1)
                sp.sem_inc(st[q], 16)
            with sp.Fori(0, PAIRS) as i:
                e = [sp.value_load(BEX[0:1, bass.ds(i * 2 + q, 1)], min_val=0, max_val=NE - 1) for q in range(2)]
                for q in range(2):
                    hold(sp, gu_free[q], i + 1)
                    for n, w in enumerate((wg, wu)):
                        sp.dma_start(WGU[:, q, :, n * ED:(n + 1) * ED],
                                     w[0, bass.ds(e[q], 1)].rearrange("e (p c) n -> p (e c) n", c=KC)).then_inc(
                                         gu_in[q], 16)
                for q in range(2):
                    hold(sp, d_free[q], i + 1)
                    sp.dma_start(WD[:, q], wd[0, bass.ds(e[q], 1)].rearrange("e (p c) n -> p (e c) n",
                                                                             c=2)).then_inc(d_in[q], 16)

        @block.gpsimd
        def _(pool):
            with pool.Fori(0, PAIRS) as i:
                for q in range(2):
                    hold(pool, idx[q], i + 1)
                    nc.gpsimd.indirect_dma_start(
                        out=G[:, q], out_offset=None, in_=xn_dram,
                        in_offset=bass.IndirectOffsetOnAxis(ap=ID[:, q], axis=0)).then_inc(g_in[q], 16)

        @block.tensor
        def _(pe):
            with pe.Fori(0, PAIRS) as i:
                for q in range(2):
                    hold(pe, g_in[q], i * 16 + 16)
                    if q == 1:
                        for s in (xa, xd):
                            hold(pe, s[0], i + 1)
                    for c in range(KC):
                        last = nc.tensor.transpose(ps[c // 4][:, (c % 4) * P:(c % 4 + 1) * P], G[:, q, c::KC], k.ident)
                    last.then_inc(turned[q], 1)
                    hold(pe, xa[q], i + 1)
                    hold(pe, xd[q], i + 1)
                    hold(pe, gu_in[q], i * 32 + 32)
                    for c in range(KC):
                        last = nc.tensor.matmul(ps[2 + q][:, :], XTT[:, q, c], WGU[:, q, c],
                                                start=(c == 0), stop=(c == KC - 1))
                    last.then_inc(up[q], 1)
                for q in range(2):
                    hold(pe, hid[q], i + 1)
                    pe.sem_inc(gu_free[q], 1)
                    if q == 1:
                        hold(pe, hto[0], i + 1)
                    for f in range(2):
                        last = nc.tensor.transpose(ps[4][:, f * P:(f + 1) * P], H[:, q, f::2], k.ident)
                    last.then_inc(ht[q], 1)
                    hold(pe, hto[q], i + 1)
                    hold(pe, d_in[q], i * 16 + 16)
                    if q == 1:
                        for s in (ya, yd):
                            hold(pe, s[0], i + 1)
                    for half in range(2):
                        for f in range(2):
                            last = nc.tensor.matmul(ps[6 + half][:, :], HT[:, q, f],
                                                    WD[:, q, f, half * 512:(half + 1) * 512],
                                                    start=(f == 0), stop=(f == 1))
                    last.then_inc(dn[q], 1)
                for q in range(2):
                    hold(pe, ya[q], i + 1)
                    hold(pe, yd[q], i + 1)
                    pe.sem_inc(d_free[q], 1)

        @block.scalar
        def _(act):
            with act.Fori(0, PAIRS) as i:
                for q in range(2):
                    hold(act, turned[q], i + 1)
                    for c in range(KC // 2):
                        last = nc.scalar.activation(XTT[:, q, c], ps[0][:, c * P:(c + 1) * P], ACT.Identity,
                                                    bias=k.add_col[1][0][:, c:c + 1],
                                                    scale=k.mul_col[1][0][:, c:c + 1])
                    last.then_inc(xa[q], 1)
                for q in range(2):
                    hold(act, up[q], i + 1)
                    nc.scalar.activation(SG[:, q], ps[2 + q][:, 0:ED], ACT.Silu).then_inc(sil[q], 1)
                for q in range(2):
                    hold(act, ht[q], i + 1)
                    nc.scalar.copy(HT[:, q], ps[4][:, 0:2 * P].rearrange("p (f n) -> p f n", f=2)).then_inc(hto[q], 1)
                    hold(act, dn[q], i + 1)
                    hold(act, st[q], i * 16 + 16)
                    nc.scalar.copy(YB[:, q, 0:512], ps[6][:, :]).then_inc(ya[q], 1)
                    hold(act, ya[q], i + 1)
                    hold(act, yd[q], i + 1)
                    act.dma_start(y_dram[bass.ds((i * 2 + q) * P, P), :], YB[:, q]).then_inc(st[q], 16)
            for q in range(2):
                act.wait_ge(st[q], 16 * PAIRS + 16)

        @block.vector
        def _(dve):
            for q in range(2):
                nc.vector.tensor_copy(ID[:, q], IDX[:, q:q + 1]).then_inc(idx[q], 1)
            with dve.Fori(0, PAIRS) as i:
                for q in range(2):
                    hold(dve, turned[q], i + 1)
                    nc.vector.tensor_copy(ID[:, q], IDX[:, bass.ds(i * 2 + 2 + q, 1)]).then_inc(idx[q], 1)
                    for c in range(KC // 2, KC):
                        last = nc.vector.tensor_scalar(XTT[:, q, c], ps[1][:, (c - 4) * P:(c - 3) * P],
                                                       k.mul_col[1][0][:, c:c + 1], k.add_col[1][0][:, c:c + 1],
                                                       ALU.mult, ALU.add)
                    last.then_inc(xd[q], 1)
                for q in range(2):
                    hold(dve, sil[q], i + 1)
                    nc.vector.tensor_tensor(H[:, q], SG[:, q], ps[2 + q][:, ED:], ALU.mult).then_inc(hid[q], 1)
                for q in range(2):
                    hold(dve, dn[q], i + 1)
                    hold(dve, st[q], i * 16 + 16)
                    nc.vector.tensor_copy(YB[:, q, 512:], ps[7][:, :]).then_inc(yd[q], 1)
    

def combine(nc, k, ctx, cr, X1, ACC, DST, WK, y_dram, final_g, out):
    sem = lambda n: ctx.semaphore("fin_" + n)
    NB = 4
    g_in, used, gain_in, vch, sq, ready, st = ([sem(f"rows_{n}") for n in range(NB)], sem("rows_used"), sem("gain"),
                                               sem("chain"), sem("squares"), sem("ready"), [sem("even_stored"), sem("odd_stored")])
    G, FG, junk = cr.take(NB, D), cr.take(D), cr.take(2, D)
    OUT = cr.take(2, D)
    ss, rs, ri = (cr.take(2, 1) for _ in range(3))
    rt = cr.take(1)
    with nc.Block() as block:
        @block.gpsimd
        def _(pool):
            for n in range(XT * TOPK):
                t, s = n // TOPK, n % TOPK
                if n >= NB:
                    pool.wait_ge(used, n - NB + 1)
                nc.gpsimd.indirect_dma_start(
                    out=G[:, n % NB], out_offset=None, in_=y_dram,
                    in_offset=bass.IndirectOffsetOnAxis(ap=DST[:, t, s:s + 1], axis=0)).then_inc(g_in[n % NB], 16)

        @block.sync
        def _(sp):
            sp.dma_start(FG, final_g.rearrange("(a n) -> a n", a=1).to_broadcast([P, D])).then_inc(gain_in, 16)
            for t in range(XT):
                sp.wait_ge(ready, t + 1)
                sp.dma_start(out[0, t * P:(t + 1) * P, :], OUT[:, t % 2]).then_inc(st[t % 2], 16)
            for s in st:
                sp.wait_ge(s, 16 * (XT // 2))

        @block.scalar
        def _(act):
            for t in range(XT):
                act.wait_ge(sq, 2 * t + 1)
                nc.scalar.activation(junk[:, t % 2], X1[:, t], ACT.Square, accum_out=ss[:, t % 2]).then_inc(sq, 1)

        @block.vector
        def _(dve):
            chain = Chain(dve, vch)
            dve.wait_ge(gain_in, 16)
            for t in range(XT):
                for s in range(TOPK):
                    n = t * TOPK + s
                    dve.wait_ge(g_in[n % NB], 16 * (n // NB + 1))
                    if s > 0:
                        dve.wait_ge(used, n)
                    nc.vector.scalar_tensor_tensor(ACC[:, t], G[:, n % NB], WK[:, t, s:s + 1], ACC[:, t],
                                                   ALU.mult, ALU.add).then_inc(used, 1)
                dve.wait_ge(used, (t + 1) * TOPK)
                chain(nc.vector.tensor_tensor(ACC[:, t], ACC[:, t], k.gate[1], ALU.mult))
                nc.vector.tensor_tensor(X1[:, t], X1[:, t], ACC[:, t], ALU.add).then_inc(sq, 1)
                dve.wait_ge(sq, 2 * t + 2)
                chain(nc.vector.tensor_scalar(rs[:, t % 2], ss[:, t % 2], 1.0 / D, RMS_EPS, ALU.mult, ALU.add))
                rsqrt(nc, chain, rs[:, t % 2], ri[:, t % 2], rt)
                if t >= 2:
                    dve.wait_ge(st[t % 2], 16 * (t // 2))
                nc.vector.scalar_tensor_tensor(OUT[:, t % 2], X1[:, t], ri[:, t % 2], FG, ALU.mult,
                                               ALU.mult).then_inc(ready, 1)


def block_kernel(nc, io, out):
    ctx = ExitStack()
    with ctx:
        k = Kernel()
        arena = ctx.enter_context(nc.sbuf_tensor("arena", [P, 52800], F32))
        k.ps = [ctx.enter_context(nc.psum_tensor(f"bank{n}", [P, 512], F32)) for n in range(8)]
        k.ps = [b[:, :] for b in k.ps]
        y_dram = nc.dram_tensor("mixed", (SEQ, D), F32, kind="Internal").ap()
        cr = Carve(arena, 0)
        k.ident, k.ones, k.ge, k.gt, k.le, k.lt = (cr.take(P) for _ in range(6))
        k.blk = {b: cr.take(P) for b in (16, 32, 64)}
        k.lvl = {b: cr.take(P) for b in (32, 64, 128)}
        k.glamask, k.glacum, k.dmask, k.dmaskT, k.cap, k.floor = ([cr.take(P) for _ in range(2)] for _ in range(6))
        k.incl, k.strictT, k.strict = [k.ge, k.le], [k.gt, k.lt], [k.lt, k.gt]
        k.gate = [cr.take(D) for _ in range(2)]
        k.mul_col = [[cr.take(KC) for _ in range(2)] for _ in range(2)]
        k.add_col = [[cr.take(KC) for _ in range(2)] for _ in range(2)]
        keep = cr.at
        k.hT = cr.take(KC, TOK)
        free = cr.at
        at = lambda a: Carve(arena, a)
        with Phase(nc) as c:
            constants(nc, k, c)
        with Phase(nc) as c:
            modulation(nc, k, c, at(keep), io["c"], io["c_ctx"], io["w_mod"], io["b_mod"], io["norm1_g"], io["norm2_g"])
        with Phase(nc) as c:
            normed_hidden(nc, k, c, at(free), io["x"], io["ctx"])
        with Phase(nc) as c:
            gla(nc, k, c, at(free), io["w_in"], io["gla_gate_w2"], io["gla_gate_b"], io["gla_norm_g"], y_dram)
        with Phase(nc) as c:
            mamba(nc, k, c, at(free), io["w_in"], io["ssm_conv_w"], io["ssm_conv_b"], io["ssm_A_log"],
                  io["ssm_dt_bias"], io["ssm_D"], io["ssm_norm_g"], y_dram)
        with Phase(nc) as c:
            deltanet(nc, k, c, at(free), io["w_in"], io["dn_conv_w"], io["dn_A_log"], io["dn_dt_bias"],
                     io["dn_norm_g"], y_dram)
        with Phase(nc) as c:
            rwkv(nc, k, c, at(free), keep, io["w_in"], io["rwkv_w_w2"], io["rwkv_w0"], io["rwkv_a_w2"], io["rwkv_a0"],
                 io["rwkv_g_w2"], io["rwkv_k_k"], io["rwkv_k_a"], io["rwkv_r_k"], io["rwkv_ln_g"], io["rwkv_ln_b"],
                 y_dram)
        X1 = at(keep).take(XT, D)
        ACC = at(keep + XT * D).take(XT, D)
        small = Carve(arena, keep + 2 * XT * D)
        SC, SB = small.take(XT, NE), small.take(XT, NE)
        DST, WK = small.take(XT, TOPK).bitcast(I32), small.take(XT, TOPK)
        BEX, IDX = small.take(NBLK).bitcast(I32), small.take(NBLK + 2).bitcast(I32)
        rest = small.at
        HT = small.take(KC, SEQ)
        xn_dram = nc.dram_tensor("normed_rows", (SEQ, D), F32, kind="Internal").ap()
        buf_dram = nc.dram_tensor("grouped_tokens", (NBLK * P, 1), I32, kind="Internal").ap()
        yb_dram = nc.dram_tensor("expert_rows", (NBLK * P, D), F32, kind="Internal").ap()
        with Phase(nc) as c:
            mixed_out(nc, k, c, at(small.at), io["x"], io["w_out"], y_dram, xn_dram, X1, HT)
        with Phase(nc) as c:
            shared_and_scores(nc, k, c, at(small.at), HT, io["router_w"], io["router_bias"], io["sh_w_gate"],
                              io["sh_w_up"], io["sh_w_down"], ACC, SC, SB)
        with Phase(nc) as c:
            dispatch(nc, k, c, at(rest), SC, SB, buf_dram, DST, WK, BEX, IDX)
        with Phase(nc) as c:
            experts(nc, k, c, at(rest), io["exp_w_gate"], io["exp_w_up"], io["exp_w_down"], xn_dram, yb_dram, BEX, IDX)
        with Phase(nc) as c:
            combine(nc, k, c, at(rest), X1, ACC, DST, WK, yb_dram, io["final_norm_g"], out)


_INS = ['x', 'c', 'ctx', 'c_ctx', 'norm1_g', 'norm2_g', 'w_mod', 'b_mod', 'w_in', 'w_out',
        'gla_gate_w2', 'gla_gate_b', 'gla_norm_g', 'rwkv_w_w2', 'rwkv_w0', 'rwkv_a_w2', 'rwkv_a0', 'rwkv_g_w2',
        'rwkv_k_k', 'rwkv_k_a', 'rwkv_r_k', 'rwkv_ln_g', 'rwkv_ln_b', 'ssm_conv_w', 'ssm_conv_b', 'ssm_A_log',
        'ssm_dt_bias', 'ssm_D', 'ssm_norm_g', 'dn_conv_w', 'dn_A_log', 'dn_dt_bias', 'dn_norm_g', 'router_w',
        'router_bias', 'exp_w_gate', 'exp_w_up', 'exp_w_down', 'sh_w_gate', 'sh_w_up', 'sh_w_down', 'final_norm_g']


def kernel(**inputs):
    import numpy as _np
    import concourse.bacc as _bacc
    from concourse import mybir as _mybir
    from concourse.bass_utils import run_bass_kernel_spmd as _run

    nc = _bacc.Bacc("TRN2", target_bir_lowering=False, num_devices=1)
    arrays, args = {}, {}
    for name in _INS:
        a = _np.ascontiguousarray(inputs[name])
        arrays[f"in_{name}_dram"] = a
        args[name] = nc.dram_tensor(f"in_{name}_dram", a.shape, _mybir.dt.from_np(a.dtype), kind="ExternalInput").ap()
    out = nc.dram_tensor("out_0_dram", (1, SEQ, D), _mybir.dt.float32, kind="ExternalOutput").ap()
    block_kernel(nc, args, out)
    r = _run(nc, [arrays], core_ids=[0])
    return r.results[0]["out_0_dram"]
```
